# Optimizing a Trainium2 kernel written in Bass

```python
import math
import jax, jax.numpy as jnp
from jax import lax
import numpy as np

D_MODEL = 1024
BATCH = 1
SEQ = 256
DEPTH = 2
DEC_BATCH = 1
DEC_SEQ = 32
PAST_LEN = 256

CHUNK = 64
N_AB_LAYERS = (DEPTH + 1) // 2
N_RET_LAYERS = DEPTH // 2
EPS = 1e-6

GLA_HEADS = 4
GLA_DK = 64
GLA_DV = 128
GLA_QK = GLA_HEADS * GLA_DK
A_WIDTH = GLA_HEADS * GLA_DV
GLA_GATE_RANK = 16
GLA_TAU = 16.0
A_COLS = 2 * GLA_QK + A_WIDTH + GLA_GATE_RANK + A_WIDTH
A_SPLITS = [GLA_QK, 2 * GLA_QK, 2 * GLA_QK + A_WIDTH, 2 * GLA_QK + A_WIDTH + GLA_GATE_RANK]

RWKV_HEADS = 8
RWKV_N = 64
B_WIDTH = RWKV_HEADS * RWKV_N
RWKV_DECAY_LORA = 64
RWKV_A_LORA = 64
RWKV_GATE_LORA = 128
RWKV_GN_EPS = 64e-5
B_COLS = 3 * B_WIDTH + RWKV_DECAY_LORA + RWKV_A_LORA + RWKV_GATE_LORA
B_SPLITS = [B_WIDTH, 2 * B_WIDTH, 3 * B_WIDTH, 3 * B_WIDTH + RWKV_DECAY_LORA,
            3 * B_WIDTH + RWKV_DECAY_LORA + RWKV_A_LORA]

RET_HEADS = 4
RET_DK = D_MODEL // RET_HEADS
RET_DV = 2 * D_MODEL // RET_HEADS
RET_QK = RET_HEADS * RET_DK
RET_V = RET_HEADS * RET_DV
RET_COLS = 2 * RET_QK + 2 * RET_V
RET_SPLITS = [RET_QK, 2 * RET_QK, 2 * RET_QK + RET_V]
RET_GN_EPS = 1e-5
ROPE_BASE = 10000.0

D_FF = 2816
N_EXPERTS = 8
TOP_K = 2

kernel_name = 'hybrid_gla_rwkv7_retention_stream_step'

def rmsnorm(x, g):
    xf = x.astype(jnp.float32)
    y = xf * lax.rsqrt(jnp.mean(xf * xf, axis=-1, keepdims=True) + EPS)
    return (y * g.astype(jnp.float32)).astype(x.dtype)

def head_groupnorm(x, g, b, eps):
    mu = jnp.mean(x, axis=-1, keepdims=True)
    var = jnp.mean(jnp.square(x - mu), axis=-1, keepdims=True)
    y = ((x - mu) * lax.rsqrt(var + eps)).reshape(*x.shape[:-2], -1)
    return y * g.astype(jnp.float32) + b.astype(jnp.float32)

def to_chunks(a, C):
    B, T, H, d = a.shape
    return a.reshape(B, T // C, C, H, d).transpose(1, 0, 3, 2, 4)

def from_chunks(o):
    nc, B, H, C, d = o.shape
    return o.transpose(1, 0, 3, 2, 4).reshape(B, nc * C, H, d)

def gla_chunked(q, k, v, logg, s0):
    T = q.shape[1]
    C = min(CHUNK, T)
    causal = jnp.tril(jnp.ones((C, C), dtype=bool))

    def step(s, inp):
        qc, kc, vc, gc = inp
        b = jnp.cumsum(gc, axis=-2)
        o_inter = jnp.einsum('bhik,bhkv->bhiv', qc * jnp.exp(b), s)
        diff = b[:, :, :, None, :] - b[:, :, None, :, :]
        decay = jnp.exp(jnp.where(causal[:, :, None], diff, -jnp.inf))
        att = jnp.einsum('bhik,bhjk,bhijk->bhij', qc, kc, decay)
        o = o_inter + jnp.einsum('bhij,bhjv->bhiv', att, vc)
        b_last = b[:, :, -1:, :]
        s_new = jnp.exp(b_last[:, :, 0, :])[..., None] * s + jnp.einsum(
            'bhjk,bhjv->bhkv', kc * jnp.exp(b_last - b), vc)
        return s_new, o

    s_fin, o = lax.scan(step, s0, (to_chunks(q, C), to_chunks(k, C), to_chunks(v, C), to_chunks(logg, C)))
    return from_chunks(o), s_fin

def retention_chunked(q, k, v, log_gamma, r0):
    T = q.shape[1]
    C = min(CHUNK, T)
    causal = jnp.tril(jnp.ones((C, C), dtype=bool))
    idx = jnp.arange(C, dtype=jnp.float32)
    b = (idx + 1.0)[None, :] * log_gamma[:, None]
    decay = jnp.exp(jnp.where(causal[None], b[:, :, None] - b[:, None, :], -jnp.inf))
    inter_scale = jnp.exp(b)[None, :, :, None]
    state_scale = jnp.exp(b[:, -1:] - b)[None, :, :, None]
    total = jnp.exp(b[:, -1])[None, :, None, None]

    def step(r, inp):
        qc, kc, vc = inp
        o_inter = jnp.einsum('bhik,bhkv->bhiv', qc, r) * inter_scale
        att = jnp.einsum('bhik,bhjk->bhij', qc, kc) * decay[None]
        o = o_inter + jnp.einsum('bhij,bhjv->bhiv', att, vc)
        r_new = total * r + jnp.einsum('bhjk,bhjv->bhkv', kc * state_scale, vc)
        return r_new, o

    r_fin, o = lax.scan(step, r0, (to_chunks(q, C), to_chunks(k, C), to_chunks(v, C)))
    return from_chunks(o), r_fin

def rwkv7_scan(r, logw, k, v, kk, a, s0):
    def step(s, inp):
        rt, wt, kt, vt, kkt, at = inp
        sa = jnp.einsum('bhij,bhj->bhi', s, -kkt)
        s = (s * jnp.exp(wt)[:, :, None, :] + sa[..., None] * (kkt * at)[:, :, None, :]
             + vt[..., None] * kt[:, :, None, :])
        y = jnp.einsum('bhij,bhj->bhi', s, rt)
        return s, y

    xs = tuple(t.transpose(1, 0, 2, 3) for t in (r, logw, k, v, kk, a))
    s_fin, y = lax.scan(step, s0, xs)
    return y.transpose(1, 0, 2, 3), s_fin

def rotary(x, pos):
    d = x.shape[-1]
    inv = 1.0 / (ROPE_BASE ** (jnp.arange(0, d, 2, dtype=jnp.float32) / d))
    ang = pos.astype(jnp.float32)[:, None] * inv[None, :]
    cos = jnp.cos(ang)[None, :, None, :]
    sin = jnp.sin(ang)[None, :, None, :]
    x1, x2 = x[..., : d // 2], x[..., d // 2:]
    return jnp.concatenate([x1 * cos - x2 * sin, x1 * sin + x2 * cos], axis=-1)

def ab_mixer(h, s_gla, s_rwkv, s_shift, w, i):
    f32 = jnp.float32
    B, T, _ = h.shape
    u = jnp.einsum('btd,dc->btc', h, w['ab_w_in'][i])
    ua, ub = u[..., :A_COLS], u[..., A_COLS:]
    qa, ka, va, ga, oga = jnp.split(ua.astype(f32), A_SPLITS, axis=-1)
    qa = qa.reshape(B, T, GLA_HEADS, GLA_DK) * (GLA_DK ** -0.5)
    ka = ka.reshape(B, T, GLA_HEADS, GLA_DK)
    va = va.reshape(B, T, GLA_HEADS, GLA_DV)
    logg = jax.nn.log_sigmoid(ga @ w['gla_w_gate2'][i].astype(f32) + w['gla_b_gate'][i].astype(f32)) / GLA_TAU
    oa, s_gla_new = gla_chunked(qa, ka, va, logg.reshape(B, T, GLA_HEADS, GLA_DK), s_gla.astype(f32))
    oa = oa * lax.rsqrt(jnp.mean(oa * oa, axis=-1, keepdims=True) + EPS) * w['gla_norm'][i].astype(f32)
    oa = oa.reshape(B, T, A_WIDTH) * jax.nn.silu(oga)
    ub_prev = jnp.concatenate([s_shift.astype(ub.dtype), ub[:, :-1]], axis=1)
    ubs = (ub + w['rwkv_mu'][i] * (ub_prev - ub)).astype(f32)
    rb, kb, vb, wl, al, gl = jnp.split(ubs, B_SPLITS, axis=-1)
    dec = -jax.nn.softplus(-(w['rwkv_w0'][i].astype(f32) + jnp.tanh(wl) @ w['rwkv_w2'][i].astype(f32))) - 0.5
    logw = -jnp.exp(dec)
    a = jax.nn.sigmoid(w['rwkv_a0'][i].astype(f32) + al @ w['rwkv_a2'][i].astype(f32))
    g = jax.nn.sigmoid(gl) @ w['rwkv_g2'][i].astype(f32)
    heads = lambda t: t.reshape(B, T, RWKV_HEADS, RWKV_N)
    kk = heads(kb * w['rwkv_k_k'][i].astype(f32))
    kk = kk / jnp.maximum(jnp.sqrt(jnp.sum(kk * kk, axis=-1, keepdims=True)), 1e-12)
    kb = kb * (1.0 + (a - 1.0) * w['rwkv_k_a'][i].astype(f32))
    rh, kh, vh = heads(rb), heads(kb), heads(vb)
    yb, s_rwkv_new = rwkv7_scan(rh, heads(logw), kh, vh, kk, heads(a), s_rwkv.astype(f32))
    bonus = jnp.sum(rh * kh * w['rwkv_r_k'][i].astype(f32), axis=-1, keepdims=True) * vh
    yb = head_groupnorm(yb, w['rwkv_gn_g'][i], w['rwkv_gn_b'][i], RWKV_GN_EPS) + bonus.reshape(B, T, B_WIDTH)
    yb = yb * g
    y = jnp.concatenate([oa, yb], axis=-1).astype(h.dtype) @ w['ab_w_out'][i]
    return y, s_gla_new.astype(h.dtype), s_rwkv_new.astype(h.dtype), ub[:, -1:]

def ret_mixer(h, pos, s_ret, w, i):
    f32 = jnp.float32
    B, T, _ = h.shape
    u = jnp.einsum('btd,dc->btc', h, w['ret_w_in'][i]).astype(f32)
    q, k, v, g = jnp.split(u, RET_SPLITS, axis=-1)
    q = rotary(q.reshape(B, T, RET_HEADS, RET_DK), pos)
    k = rotary(k.reshape(B, T, RET_HEADS, RET_DK), pos) * (RET_DK ** -0.5)
    v = v.reshape(B, T, RET_HEADS, RET_DV)
    log_gamma = jnp.log1p(-jnp.exp2(-5.0 - jnp.arange(RET_HEADS, dtype=f32)))
    o, s_new = retention_chunked(q, k, v, log_gamma, s_ret.astype(f32))
    o = head_groupnorm(o, w['ret_gn_g'][i], w['ret_gn_b'][i], RET_GN_EPS)
    y = (jax.nn.silu(g) * o).astype(h.dtype) @ w['ret_w_out'][i]
    return y, s_new.astype(h.dtype)

def swiglu(h, w1, w3, w2):
    return (jax.nn.silu(h @ w1) * (h @ w3)) @ w2

def moe_swiglu(h, router, w1, w3, w2):
    probs = jax.nn.softmax((h @ router).astype(jnp.float32), axis=-1)
    top_p, top_i = lax.top_k(probs, TOP_K)
    top_p = top_p / jnp.sum(top_p, axis=-1, keepdims=True)
    gates = jnp.sum(jax.nn.one_hot(top_i, N_EXPERTS, dtype=jnp.float32) * top_p[..., None], axis=-2)
    gates = gates.astype(h.dtype)
    out = jnp.zeros_like(h)
    for e in range(N_EXPERTS):
        out = out + gates[..., e:e + 1] * swiglu(h, w1[e], w3[e], w2[e])
    return out

def trunk(x, pos, st_gla, st_rwkv, st_shift, st_ret, w):
    new_gla, new_rwkv, new_shift, new_ret = [], [], [], []
    for layer in range(DEPTH):
        i = layer // 2
        h = rmsnorm(x, w['norm_mix'][layer])
        if layer % 2 == 0:
            y, sg, sr, ss = ab_mixer(h, st_gla[i], st_rwkv[i], st_shift[i], w, i)
            new_gla.append(sg)
            new_rwkv.append(sr)
            new_shift.append(ss)
            x = x + y
            x = x + swiglu(rmsnorm(x, w['norm_ffn'][layer]), w['ffn_w1'][i], w['ffn_w3'][i], w['ffn_w2'][i])
        else:
            y, st = ret_mixer(h, pos, st_ret[i], w, i)
            new_ret.append(st)
            x = x + y
            x = x + moe_swiglu(rmsnorm(x, w['norm_ffn'][layer]), w['moe_router'][i],
                               w['moe_w1'][i], w['moe_w3'][i], w['moe_w2'][i])
    y = rmsnorm(x, w['norm_final'])
    return y, jnp.stack(new_gla), jnp.stack(new_rwkv), jnp.stack(new_shift), jnp.stack(new_ret)

def setup_inputs(seed: int = 0) -> dict:
    key = jax.random.key(seed)
    ks = iter(jax.random.split(key, 64))
    f32 = jnp.float32
    nrm = lambda shape, scale: jax.random.normal(next(ks), shape, f32) * scale
    uni = lambda shape, lo, hi: jax.random.uniform(next(ks), shape, f32, lo, hi)
    NA, NR = N_AB_LAYERS, N_RET_LAYERS
    return {
        'x_prompt': nrm((BATCH, SEQ, D_MODEL), 1.0),
        'x_sample': nrm((DEC_BATCH, DEC_SEQ, D_MODEL), 1.0),
        'state_gla': nrm((NA, DEC_BATCH, GLA_HEADS, GLA_DK, GLA_DV), 0.3),
        'state_rwkv': nrm((NA, DEC_BATCH, RWKV_HEADS, RWKV_N, RWKV_N), 0.3),
        'state_shift': nrm((NA, DEC_BATCH, 1, B_COLS), 1.0),
        'state_ret': nrm((NR, DEC_BATCH, RET_HEADS, RET_DK, RET_DV), 0.3),
        'norm_mix': 1.0 + nrm((DEPTH, D_MODEL), 0.02),
        'norm_ffn': 1.0 + nrm((DEPTH, D_MODEL), 0.02),
        'norm_final': 1.0 + nrm((D_MODEL,), 0.02),
        'ab_w_in': nrm((NA, D_MODEL, A_COLS + B_COLS), D_MODEL ** -0.5),
        'ab_w_out': nrm((NA, A_WIDTH + B_WIDTH, D_MODEL), (A_WIDTH + B_WIDTH) ** -0.5),
        'gla_w_gate2': nrm((NA, GLA_GATE_RANK, GLA_QK), GLA_GATE_RANK ** -0.5),
        'gla_b_gate': 2.0 + nrm((NA, GLA_QK), 0.5),
        'gla_norm': 1.0 + nrm((NA, GLA_DV), 0.02),
        'rwkv_mu': uni((NA, B_COLS), 0.0, 1.0),
        'rwkv_w0': uni((NA, B_WIDTH), -3.0, 0.5),
        'rwkv_w2': nrm((NA, RWKV_DECAY_LORA, B_WIDTH), 0.1 * RWKV_DECAY_LORA ** -0.5),
        'rwkv_a0': nrm((NA, B_WIDTH), 0.5),
        'rwkv_a2': nrm((NA, RWKV_A_LORA, B_WIDTH), 0.3 * RWKV_A_LORA ** -0.5),
        'rwkv_g2': nrm((NA, RWKV_GATE_LORA, B_WIDTH), RWKV_GATE_LORA ** -0.5),
        'rwkv_k_k': 0.85 + nrm((NA, B_WIDTH), 0.05),
        'rwkv_k_a': 1.0 + nrm((NA, B_WIDTH), 0.05),
        'rwkv_r_k': nrm((NA, RWKV_HEADS, RWKV_N), 0.1),
        'rwkv_gn_g': 1.0 + nrm((NA, B_WIDTH), 0.02),
        'rwkv_gn_b': nrm((NA, B_WIDTH), 0.02),
        'ret_w_in': nrm((NR, D_MODEL, RET_COLS), D_MODEL ** -0.5),
        'ret_gn_g': 1.0 + nrm((NR, RET_V), 0.02),
        'ret_gn_b': nrm((NR, RET_V), 0.02),
        'ret_w_out': nrm((NR, RET_V, D_MODEL), RET_V ** -0.5),
        'ffn_w1': nrm((NA, D_MODEL, D_FF), D_MODEL ** -0.5),
        'ffn_w3': nrm((NA, D_MODEL, D_FF), D_MODEL ** -0.5),
        'ffn_w2': nrm((NA, D_FF, D_MODEL), D_FF ** -0.5),
        'moe_router': nrm((NR, D_MODEL, N_EXPERTS), D_MODEL ** -0.5),
        'moe_w1': nrm((NR, N_EXPERTS, D_MODEL, D_FF), D_MODEL ** -0.5),
        'moe_w3': nrm((NR, N_EXPERTS, D_MODEL, D_FF), D_MODEL ** -0.5),
        'moe_w2': nrm((NR, N_EXPERTS, D_FF, D_MODEL), D_FF ** -0.5),
    }

def reference(x_prompt, x_sample, state_gla, state_rwkv, state_shift, state_ret,
              norm_mix, norm_ffn, norm_final,
              ab_w_in, ab_w_out, gla_w_gate2, gla_b_gate, gla_norm,
              rwkv_mu, rwkv_w0, rwkv_w2, rwkv_a0, rwkv_a2, rwkv_g2, rwkv_k_k, rwkv_k_a, rwkv_r_k,
              rwkv_gn_g, rwkv_gn_b,
              ret_w_in, ret_gn_g, ret_gn_b, ret_w_out,
              ffn_w1, ffn_w3, ffn_w2,
              moe_router, moe_w1, moe_w3, moe_w2):
    w = {
        'norm_mix': norm_mix, 'norm_ffn': norm_ffn, 'norm_final': norm_final,
        'ab_w_in': ab_w_in, 'ab_w_out': ab_w_out, 'gla_w_gate2': gla_w_gate2,
        'gla_b_gate': gla_b_gate, 'gla_norm': gla_norm,
        'rwkv_mu': rwkv_mu, 'rwkv_w0': rwkv_w0, 'rwkv_w2': rwkv_w2, 'rwkv_a0': rwkv_a0,
        'rwkv_a2': rwkv_a2, 'rwkv_g2': rwkv_g2, 'rwkv_k_k': rwkv_k_k, 'rwkv_k_a': rwkv_k_a,
        'rwkv_r_k': rwkv_r_k, 'rwkv_gn_g': rwkv_gn_g, 'rwkv_gn_b': rwkv_gn_b,
        'ret_w_in': ret_w_in, 'ret_gn_g': ret_gn_g, 'ret_gn_b': ret_gn_b, 'ret_w_out': ret_w_out,
        'ffn_w1': ffn_w1, 'ffn_w3': ffn_w3, 'ffn_w2': ffn_w2,
        'moe_router': moe_router, 'moe_w1': moe_w1, 'moe_w3': moe_w3, 'moe_w2': moe_w2,
    }
    bp, tp = x_prompt.shape[0], x_prompt.shape[1]
    dt = x_prompt.dtype
    z_gla = jnp.zeros((N_AB_LAYERS, bp, GLA_HEADS, GLA_DK, GLA_DV), dt)
    z_rwkv = jnp.zeros((N_AB_LAYERS, bp, RWKV_HEADS, RWKV_N, RWKV_N), dt)
    z_shift = jnp.zeros((N_AB_LAYERS, bp, 1, B_COLS), dt)
    z_ret = jnp.zeros((N_RET_LAYERS, bp, RET_HEADS, RET_DK, RET_DV), dt)
    pos_prompt = jnp.arange(tp)
    pos_sample = PAST_LEN + jnp.arange(x_sample.shape[1])
    y_prompt, p_gla, p_rwkv, p_shift, p_ret = trunk(x_prompt, pos_prompt, z_gla, z_rwkv, z_shift, z_ret, w)
    y_sample, s_gla, s_rwkv, s_shift, s_ret = trunk(x_sample, pos_sample, state_gla, state_rwkv,
                                                    state_shift, state_ret, w)
    return (y_prompt, y_sample, p_gla, p_rwkv, p_shift, p_ret, s_gla, s_rwkv, s_shift, s_ret)


_drawn_inputs = setup_inputs


def setup_inputs(seed=0):
    import zlib

    import numpy as np

    out = dict(_drawn_inputs(seed))
    spreads = {}
    factors = {'norm_final': 2.964, 'gla_norm': 2.916, 'rwkv_w2': 5.53, 'rwkv_gn_g': 2.703}
    for name, (base, spread) in spreads.items():
        noise = np.random.default_rng([zlib.crc32(name.encode()), seed]).standard_normal(out[name].shape)
        drawn = base * np.exp(spread * noise) if base else spread * noise
        out[name] = __import__('jax').numpy.asarray(drawn.astype(out[name].dtype))
    for name, factor in factors.items():
        out[name] = (out[name] * factor).astype(out[name].dtype)
    return out
```

```python
from contextlib import ExitStack

import numpy as np
import concourse.bass as bass
from concourse import mybir
from concourse.alu_op_type import AluOpType as ALU

ACT = mybir.ActivationFunctionType
F32 = mybir.dt.float32
I32 = mybir.dt.int32
AX_X = mybir.AxisListType.X

P = 128
D, KD = 1024, 8
TP, TS = 256, 32
T = TP + TS
C = 32
NCH = T // C
GROUPS = [(0, 128), (128, 128), (256, 32)]
DFF = 2816
KF = DFF // P
NEXP = 8
QA, KA, VA, GA, OGA = 0, 256, 512, 1024, 1040
B0 = 1552
RB, KB, VB, LORA = B0, B0 + 512, B0 + 1024, B0 + 1536
RING = 3
RINGX = 11
CAP = 112
EPS = 1e-6
SMALL_LOADS = 8


def const_layout():
    at, n = {}, 0
    for name, w in (("ident", 128), ("ones", 128), ("heads", 128), ("incl_t", 256), ("strict_incl_t", 256),
                    ("strict", 128), ("scan", T), ("chunk", 4), ("ident64", 64), ("cos", T), ("sin", T),
                    ("ret_mask", 4 * 256), ("ret_k", 3 * 4), ("ret_q", 4 * 32), ("cols", 128), ("before", 128)):
        at[name] = (n, w)
        n += w
    return at, n


def const_array():
    at, n = const_layout()
    c = np.zeros((P, n), np.float32)

    def put(name, a):
        o, w = at[name]
        c[:, o:o + w] = np.asarray(a, np.float64).reshape(P, w).astype(np.float32)

    i = np.arange(P)
    same = (i[:, None] // C) == (i[None, :] // C)
    put("ident", np.eye(P))
    put("ones", np.ones((P, P)))
    put("heads", (i[:, None] // 64) == (i[None, :] // 64))
    incl_t = same & (i[:, None] <= i[None, :])
    strict_t = same & (i[:, None] < i[None, :])
    put("incl_t", np.concatenate([incl_t, incl_t], 1))
    put("strict_incl_t", np.concatenate([strict_t, incl_t], 1))
    put("strict", same & (i[:, None] > i[None, :]))
    put("scan", np.tile((np.arange(T) % C != 0)[None], (P, 1)))
    put("chunk", (i[:, None] // C) == np.arange(4)[None])
    put("ident64", (i[:, None] % 64) == np.arange(64)[None])
    inv = (1.0 / (np.float32(10000.0) ** (np.arange(0, 256, 2, dtype=np.float32) / np.float32(256)))).astype(np.float32)
    ang = (inv[:, None] * np.arange(T, dtype=np.float32)[None]).astype(np.float32).astype(np.float64)
    put("cos", np.cos(ang))
    put("sin", np.sin(ang))
    gam = 1.0 - 2.0 ** (-5.0 - np.arange(4))
    d = np.arange(256)[None, :] - i[:, None]
    put("ret_mask", np.stack([np.where(d >= 0, g ** np.maximum(d, 0), 0) / 16 for g in gam], 1))
    last = np.array([255, 127, 31])
    k = np.zeros((P, 3, 4))
    for g in range(3):
        k[:, g, :] = gam[None] ** np.maximum(last[g] - i, 0)[:, None] / 16
    put("ret_k", k)
    put("ret_q", np.tile((gam[:, None] ** (np.arange(32)[None] + 1)).reshape(1, -1), (P, 1)))
    put("cols", np.tile(np.arange(P)[None], (P, 1)))
    put("before", i[:, None] < i[None, :])
    return c


ROWS = [("norm_mix", 16), ("norm_ffn", 16), ("norm_final", 8), ("gla_b_gate", 2), ("gla_norm", 1), ("rwkv_mu", 14),
        ("rwkv_w0", 4), ("rwkv_a0", 4), ("rwkv_k_k", 4), ("rwkv_k_a", 4), ("rwkv_r_k", 4), ("rwkv_gn_g", 4),
        ("rwkv_gn_b", 4), ("state_shift", 14), ("ret_gn_g", 16), ("ret_gn_b", 16)]
VEC = {}
_n = 0
for _name, _w in ROWS:
    if _name == "ret_gn_g":
        _n = P
    VEC[_name] = (_n, _w)
    _n += _w
NVEC = _n


class Tally:

    def __init__(self, sem, name=""):
        self.sem, self.name, self.base, self.k, self.i, self.per = sem, name, 0, 0, None, 0

    def enter(self, i, per):
        self.base, self.k, self.i, self.per = self.base + self.k, 0, i, per

    def leave(self, n):
        assert self.k in (0, self.per), (self.name, self.k, self.per)
        self.base, self.k, self.i = self.base + self.per * n, 0, None

    def value(self, d=0):
        v = self.base + self.k + d
        return v if self.i is None else self.i * self.per + v

    def low(self, d=0):
        return self.base + self.k + d

    def made(self, ins, n=1):
        ins.then_inc(self.sem, n)
        self.k += n
        return ins

    def wait(self, eng, d=0):
        eng.wait_ge(self.sem, self.value(d))

    def next(self, eng, n=1):
        self.k += n
        eng.wait_ge(self.sem, self.value())

    def link(self, eng, ins):
        self.made(ins)
        eng.wait_ge(self.sem, self.value())

SEMAPHORES = """
    unit_used slot_free ret_stored rounds_known squares square_sums normed in_const in_rows vec_turned in_x
    x_copied x_turned first_block in_lora ga_block gate_in gate_blocks lora_in gate_out lora_out lora_mixed
    gla_evac gla_feats gla_scores gla_turned gla_vt gla_kx gla_updates gla_masked gla_states gla_o gla_osq
    gla_osum gla_read rw_evac rw_ksq rw_ksum rw_state_in rw_state_turned rw_feats rw_turned rw_plain
    rw_state_put rw_tok rw_bkx rw_scores rw_scored rw_q rw_squared rw_power rw_grown rw_grow rw_akv rw_x rw_gh
    rw_ghs rw_mn rw_z rw_yi rw_mns rw_state rw_step rw_zs rw_ys rw_final rw_y rw_mean rw_ysq rw_var rw_read
    shifts_turned mixed abo_added ffn_silu ffn_made ffn_added ret_done ret_evac ret_vturned ret_rotated
    ret_kturned ret_scores ret_vtok ret_ktok ret_att ret_state_in ret_o ret_states ret_stated_p ret_stated_s
    ret_osb ret_mean ret_osq ret_var reto_added logits frames_turned picked placed frames_tok x_taken x_added
    x_out x_give x_h x_read x_y x_ready y_turned roots eps_set lora_raw lora_shifted act_chain gate_log
    gate_sums gate_exps decay_sums decay_exps gla_og gla_root rw_kroot rw_yis rw_out rw_centred rw_root
    shifts_out ret_buffer ret_centred ret_root logits_centred logits_exp x_silu y_copied y_stored dve_chain
    places_moved stored
"""

GLA_PER = dict(unit_used=6, gla_evac=6, gla_feats=1, gla_scores=1, gla_turned=3, gla_vt=3, gla_kx=3, gla_updates=3,
               gla_masked=1, gla_states=1, gla_o=1, gla_osq=1, gla_osum=1, gla_read=1, gla_og=1, gla_root=1, dve_chain=12)
RW_PER = dict(unit_used=3, rw_evac=3, rw_ksq=1, rw_ksum=1, rw_state_in=1, rw_state_turned=1, rw_feats=1, rw_turned=3,
              rw_plain=1, rw_state_put=1, rw_tok=3, rw_bkx=3, rw_scores=3, rw_scored=3, rw_q=1, rw_squared=12, rw_power=12,
              rw_grow=12, rw_grown=12, rw_akv=1, rw_x=1, rw_gh=1, rw_ghs=1, rw_mn=3, rw_z=1, rw_yi=1, rw_mns=3, rw_step=8,
              rw_state=9, rw_zs=1, rw_ys=1, rw_final=1, rw_y=1, rw_mean=1, rw_ysq=1, rw_var=1, rw_read=1, rw_kroot=1,
              rw_yis=1, rw_out=1, rw_centred=1, rw_root=1, dve_chain=17)
FFN_PER = dict(unit_used=6, first_block=6, ffn_made=6, ffn_silu=6)
DOWN_PER = dict(unit_used=3)
RET_PER = dict(unit_used=6, first_block=6, ret_done=1, ret_evac=12, ret_vturned=1, ret_rotated=1, ret_kturned=1, ret_scores=1,
               ret_vtok=1, ret_ktok=1, ret_att=1, ret_state_in=16, ret_o=1, ret_states=1, ret_stated_p=1, ret_stated_s=1, ret_osb=1, ret_mean=1,
               ret_osq=1, ret_var=1, ret_centred=1, ret_root=1, ret_buffer=1, dve_chain=5)
X_PER = dict(x_give=1, x_taken=1, x_h=1, x_read=11, slot_free=33, x_y=1, x_added=8, x_out=8, x_silu=11)


def program(nc, a, o):
    with ExitStack() as ctx:
        layer0 = ExitStack()

        def sb(name, shape, where=ctx, dt=F32):
            return where.enter_context(nc.sbuf_tensor(name, shape, dt))

        ps = ctx.enter_context(nc.psum_tensor("ps", [P, 8, 512], F32))

        sem = {}
        for name in SEMAPHORES.split():
            sem[name] = ctx.enter_context(nc.semaphore(name))
        x_arrived = [ctx.enter_context(nc.semaphore(f"expert_weights_arrived_{s}")) for s in range(RINGX)]
        arrived = [ctx.enter_context(nc.semaphore(f"weights_arrived_{s}")) for s in range(RING)]

        ring = sb("ring", [P, RING, KD * 256])
        const = sb("const", [P, const_layout()[1]])
        rows = sb("rows", [P, 2, P])
        vec = sb("vec", [P, NVEC])
        omka = sb("omka", [P, 4])
        xT = sb("xT", [P, KD, T])
        hT = sb("hT", [P, KD, T])
        yT = sb("yT", [P, KD, T])
        rstd = sb("rstd", [P, 2, T])
        w_router = sb("w_router", [P, KD, NEXP])

        def K(name, lo=0, n=None):
            at, w = const_layout()[0][name]
            return const[:, at + lo:at + (w if n is None else lo + n)]

        def V(name, j=0, n=1):
            return vec[:, VEC[name][0] + j:VEC[name][0] + j + n]

        epsb = sb("epsb", [P, 8])

        def eps(e):
            return epsb[:, (EPS, 64e-5, None, 1e-5).index(e):][:, 0:1]

        def one():
            return epsb[:, 2:3]

        def chunks(ap):
            return ap.rearrange("p (c t) -> p c t", t=C)

        shifto = sb("shifto", [28, P])
        gla_out = sb("gla_out", [P, 2, 2, P])
        rw_out = sb("rw_out", [P, 4, 2, 64])
        L = layer0
        w_ga = sb("w_ga", [P, KD, 16], L)
        w_gate = sb("w_gate", [16, 256], L)
        w_wa = sb("w_wa", [P, 512], L)
        w_g = sb("w_g", [P, 512], L)
        lora = sb("lora", [P, 6, T], L)
        gaT = sb("gaT", [16, T], L)
        gend = sb("gend", [P, 2, NCH], L)
        lw = sb("lw", [P, 4, T], L)
        rexp = sb("rexp", [P, 3, 4, T], L)
        av = sb("av", [P, 4, T], L)
        gv = sb("gv", [P, 4, T], L)
        shiftb = sb("shiftb", [P, 2, 14], L)
        gla_in = sb("gla_in", [P, 2, P], L)
        rw_in = sb("rw_in", [P, 4, 64], L)
        G = ExitStack()
        xrow = sb("xrow", [P, 3, D], G)
        gz = sb("gz", [P, 3, 2, T], G)
        gexp = sb("gexp", [P, 4, 2, T], G)
        gx = sb("gx", [P, 6, T], G)
        gf = sb("gf", [P, 4, T], G)
        gatt = sb("gatt", [P, 2, T], G)
        gvt = sb("gvt", [P, 3, 2, P], G)
        gkx = sb("gkx", [P, 3, 4, P], G)
        gst = sb("gst", [P, 11, P], G)
        go = sb("go", [P, 4, T], G)
        G.close()
        rx = sb("rx", [P, 3, T], L)
        rp = sb("rp", [P, 3, T], L)
        rsh = sb("rsh", [P, 3, T], L)
        rt = sb("rt", [P, 5, T], L)
        rkk = sb("rkk", [P, T], L)
        rkn = sb("rkn", [P, T], L)
        rar = sb("rar", [P, 2, T], L)
        rbk = sb("rbk", [P, 2, T], L)
        rsc = sb("rsc", [P, 3, 2, 2, 256], L)
        rpw = sb("rpw", [P, 2, 3, 2, 2, P], L)
        rq = sb("rq", [P, 2, 3, 2, P], L)
        rvt = sb("rvt", [P, 3, P], L)
        rax = sb("rax", [P, 3, 2, 2, 64], L)
        rbx = sb("rbx", [P, 3, 4, P], L)
        rkx = sb("rkx", [P, 3, 4, P], L)
        rgh = sb("rgh", [P, 3, 2, P], L)
        rmt = sb("rmt", [P, NCH, P], L)
        rnw = sb("rnw", [P, NCH, P], L)
        rz = sb("rz", [P, T], L)
        ryi = sb("ryi", [P, T], L)
        rst = sb("rst", [P, 11, P], L)
        rsi = sb("rsi", [P, P], L)
        L.close()
        F = ExitStack()
        gT = sb("gT", [P, KF, T], F)
        fsil = sb("fsil", [P, 2, T], F)
        F.close()
        R = ExitStack()
        yR = sb("yR", [P, 16, T], R)
        rqk = sb("rqk", [P, 4, T], R)
        rvf = sb("rvf", [P, 4, T], R)
        rgf = sb("rgf", [P, 4, T], R)
        rrot = sb("rrot", [P, 4, T], R)
        rrt = sb("rrt", [P, 4, T], R)
        rqs = sb("rqs", [P, 2, TS], R)
        rV = sb("rV", [P, 3, 512], R)
        rK = sb("rK", [P, 3, 256], R)
        ratt = sb("ratt", [P, 416], R)
        ro = sb("ro", [P, 4, T], R)
        rosq = sb("rosq", [P, 4, T], R)
        rS0 = sb("rS0", [P, 2, 512], R)
        rS = sb("rS", [P, 2, 2, 512], R)
        R.close()
        X = ExitStack()
        xring = sb("xring", [P, RINGX, KD * 256], X)
        htok = sb("htok", [P, 3, D], X)
        top = sb("top", [P, 3, 8], X)
        topi = sb("topi", [P, 3, 8], X, mybir.dt.uint32)
        topf = sb("topf", [P, 3, 8], X)
        prob = sb("prob", [P, 3, NEXP], X)
        pick = sb("pick", [P, 3, NEXP + 1], X)
        gate = sb("gate", [P, 3, NEXP], X)
        place = sb("place", [P, 3, NEXP + 1], X)
        small = sb("small", [P, 16], X)
        counts = sb("counts", [P, NEXP], X)
        rounds = sb("rounds", [1, 1], X, I32)
        take_f = sb("take_f", [P, 3, CAP], X)
        give_f = sb("give_f", [P, 3, CAP], X)
        giveT = sb("giveT", [CAP, T], X)
        hx = sb("hx", [P, KD, CAP], X)
        gx_ = sb("gx_", [P, KF, CAP], X)
        xsil = sb("xsil", [P, 2, 2 * CAP], X)
        yx = sb("yx", [CAP, D], X)
        X.close()
        ytok = htok

        W_IN = a["ab_w_in"][0].rearrange("(k p) n -> p k n", p=P)
        W_OUT = a["ab_w_out"][0].rearrange("(k p) n -> p k n", p=P)
        W1, W3, W2, W_RET, W_RETO = (a[n][0].rearrange("(k p) n -> p k n", p=P) for n in ("ffn_w1", "ffn_w3", "ffn_w2", "ret_w_in", "ret_w_out"))
        X1, X3, X2 = (a[n][0].rearrange("e (k p) n -> e p k n", p=P) for n in ("moe_w1", "moe_w3", "moe_w2"))

        def norm_columns(r):
            return [V("norm_mix", 0, 8), V("norm_ffn", 0, 8), V("norm_mix", 8, 8), V("norm_ffn", 8, 8), V("norm_final", 0, 8)][r]

        def count_rounds(eng):
            return eng.value_load(rounds[0:1, 0:1], min_val=1, max_val=-(-T // CAP))

        block = ctx.enter_context(nc.Block())

        @block.sync
        def _(sp):
            used = Tally(sem["unit_used"], "unit_used")
            unit = [0, None, 0]

            def load(parts):
                sent, i, per = unit
                if sent >= RING or i is not None:
                    need = max(sent - RING + 1, 1)
                    sp.wait_ge(sem["unit_used"], need if i is None else i * per + need)
                slot = sent % RING
                for n, (dst, src) in enumerate(parts):
                    sp.dma_start(dst(slot), src).then_inc(arrived[slot], 16)
                unit[0] += 1

            def columns(w, c0, n, k0=0):
                return [(lambda s: ring[:, s, 0:KD * n].rearrange("p (k n) -> p k n", k=KD), w[:, k0:k0 + KD, bass.ds(c0, n)])]

            load(columns(W_IN, LORA, 256))
            with sp.Fori(0, 2) as i:
                unit[1:] = [i, 6]
                for c in (QA, KA):
                    load(columns(W_IN, i * 128 + c, 128))
                for c in (VA, VA + 128, OGA, OGA + 128):
                    load(columns(W_IN, i * 256 + c, 128))
            unit[:] = [unit[0] + 6, None, 0]
            with sp.Fori(0, 4) as i:
                unit[1:] = [i, 3]
                for c in (RB, KB, VB):
                    load(columns(W_IN, i * 128 + c, 128))
            unit[:] = [unit[0] + 9, None, 0]
            for j in range(4):
                load(columns(W_OUT, 256 * j, 256))

            for j in range(2):
                load(columns(W1, 256 * j, 256))
                load(columns(W3, 256 * j, 256))
            with sp.Fori(0, 3) as i:
                unit[1:] = [i, 18 // 3]
                for q in range(3):
                    load(columns(W1, i * 768 + (512 + 256 * q), 256))
                    load(columns(W3, i * 768 + (512 + 256 * q), 256))
            unit[:] = [unit[0] + 12, None, 0]

            def down(k, half):
                return [(lambda s: ring[:, s, 0:1024].rearrange("p (k n) -> p k n", k=2), W2[:, k, 512 * half:512 * half + 512])]

            for half in range(2):
                load(down(slice(0, 2), half))
                with sp.Fori(0, 3) as i:
                    unit[1:] = [i, 3]
                    for q in range(3):
                        load(down(bass.ds(i * 6 + (2 + 2 * q), 2), half))
                unit[:] = [unit[0] + 6, None, 0]
                load(down(slice(20, 22), half))
            with sp.Fori(0, 4) as i:
                unit[1:] = [i, 6]
                for c in (0, 1024):
                    load(columns(W_RET, i * 256 + c, 256))
                for c in (2048, 2304, 4096, 4352):
                    load(columns(W_RET, i * 512 + c, 256))
            unit[:] = [unit[0] + 18, None, 0]
            for j in range(4):
                for kh in range(2):
                    load(columns(W_RETO, 256 * j, 256, KD * kh))
            sp.wait_ge(sem["slot_free"], RINGX)
            sp.wait_ge(sem["ret_stored"], 32 * 4)
            sp.wait_ge(sem["rounds_known"], 1)
            with sp.Fori(0, count_rounds(sp)) as r:
                with sp.Fori(0, NEXP) as e:
                    turn = r * NEXP + e
                    for k in range(33):
                        sp.wait_ge(sem["slot_free"], turn * 33 + (k + 1))
                        if k < 22:
                            w = X3 if k % 2 else X1
                            dst = xring[:, k % RINGX, :].rearrange("p (k n) -> p k n", k=KD)
                            src = w[bass.ds(e, 1), :, :, 256 * (k // 2):256 * (k // 2) + 256][0]
                        else:
                            dst = xring[:, k % RINGX, :].rearrange("p (k n) -> p k n", k=2)
                            src = X2[bass.ds(e, 1), :, 2 * (k - 22):2 * (k - 22) + 2, :][0]
                        sp.dma_start(dst, src).then_inc(x_arrived[k % RINGX], 16)

        @block.tensor
        def _(pe):
            t = {n: Tally(s, n) for n, s in sem.items()}
            unit = [0, None, 0]

            def take():
                k, i, per = unit
                v = 16 * (k // RING + 1)
                pe.wait_ge(arrived[k % RING], v if i is None else i * (16 * per // RING) + v)
                unit[0] += 1
                return k % RING

            def gemm(out, slot, c0, width, rhs, start=True, stop=True, ks=KD, m=P):
                w = ring[:, slot, 0:ks * width].rearrange("p (k n) -> p k n", k=ks)
                for k in range(ks):
                    ins = nc.tensor.matmul(out, w[:, k, c0:c0 + m], rhs[:, k, :], start=start and k == 0, stop=stop and k == ks - 1)
                return ins

            def enter(i, per, units):
                for n, p in per.items():
                    t[n].enter(i, p)
                unit[1:] = [i, units]

            def leave(n, per):
                for name in per:
                    t[name].leave(n)
                unit[0] += (n - 1) * unit[2]
                unit[1:] = [None, 0]

            def norm():
                t["squares"].next(pe)
                for k in range(KD):
                    ins = nc.tensor.matmul(ps[:, 7, 0:T], K("ones"), yT[:, k, :], start=k == 0, stop=k == KD - 1)
                t["square_sums"].made(ins)
                t["normed"].next(pe)

            pe.wait_ge(sem["in_const"], 16)
            pe.wait_ge(sem["in_rows"], 16 * len(ROWS))
            nc.tensor.transpose(ps[:, 0, 0:99], rows[0:99, 0, :], K("ident")[0:99, 0:99])
            t["vec_turned"].made(nc.tensor.transpose(ps[:, 1, 0:32], rows[0:32, 1, :], K("ident")[0:32, 0:32]))
            pe.wait_ge(sem["in_x"], 48)
            for k in range(KD):
                if k >= 4:
                    pe.wait_ge(sem["x_copied"], k - 3)
                for g, (g0, n) in enumerate(GROUPS):
                    ins = nc.tensor.transpose(ps[:, 2 + k % 4, g0:g0 + n], xrow[0:n, g, k * P:(k + 1) * P], K("ident")[0:n, 0:n])
                t["x_turned"].made(ins)
            norm()

            s = take()
            t["first_block"].made(gemm(ps[:, 0, 0:T], s, 0, 256, hT))
            t["unit_used"].made(gemm(ps[:, 1, 0:T], s, 128, 256, hT))
            pe.wait_ge(sem["in_lora"], 16 * SMALL_LOADS)
            for k in range(KD):
                ins = nc.tensor.matmul(ps[0:16, 2, 0:T], w_ga[:, k, :], hT[:, k, :], start=k == 0, stop=k == KD - 1)
            t["ga_block"].made(ins)
            t["gate_in"].next(pe)
            for j in range(2):
                ins = nc.tensor.matmul(ps[:, 3 + j, 0:T], w_gate[:, j * P:(j + 1) * P], gaT[:, :], start=True, stop=True)
            t["gate_blocks"].made(ins)
            t["lora_in"].next(pe)
            for j in range(4):
                b = 3 * (j % 2)
                if j == 1:
                    pe.wait_ge(sem["gate_out"], 1)
                if j >= 2:
                    pe.wait_ge(sem["lora_out"], j - 1)
                nc.tensor.matmul(ps[:, b, 0:T], w_wa[0:64, j * P:(j + 1) * P], lora[0:64, 4, :], start=True, stop=True)
                nc.tensor.matmul(ps[:, b + 1, 0:T], w_wa[64:128, j * P:(j + 1) * P], lora[64:128, 4, :], start=True, stop=True)
                t["lora_mixed"].made(nc.tensor.matmul(ps[:, b + 2, 0:T], w_g[:, j * P:(j + 1) * P], lora[:, 5, :], start=True, stop=True))
            t["lora_out"].k = 4
            t["lora_out"].wait(pe)

            with pe.Fori(0, 2) as i:
                enter(i, GLA_PER, 6)
                for b in range(6):
                    if b >= 2:
                        t["gla_evac"].wait(pe, b - 1)
                    s = take()
                    t["unit_used"].made(gemm(ps[:, b % 2, 0:T], s, 0, 128, hT))
                t["gla_evac"].k += 6
                t["gla_feats"].next(pe)
                for h in range(2):
                    for g, (g0, n) in enumerate(GROUPS):
                        r = slice(64 * h, 64 * h + 64)
                        ins = nc.tensor.matmul(ps[0:n, 2 + h, g0:g0 + n], gf[r, 1, g0:g0 + n], gf[r, 0, g0:g0 + n], start=True, stop=True)
                t["gla_scores"].made(ins)
                t["gla_evac"].wait(pe)
                for g, (g0, n) in enumerate(GROUPS):
                    for j, src in enumerate((gf[:, 3, g0:g0 + n], gx[:, 2, g0:g0 + n], gx[:, 3, g0:g0 + n])):
                        ins = nc.tensor.transpose(ps[0:n, 4 + g, j * P:(j + 1) * P], src, K("ident"))
                    t["gla_turned"].made(ins)
                for g, (g0, n) in enumerate(GROUPS):
                    t["gla_vt"].next(pe)
                    t["gla_kx"].next(pe)
                    b = (7, 4, 5)[g]
                    for h in range(2):
                        for c in range(n // C):
                            ins = nc.tensor.matmul(ps[64 * h:64 * h + 64, b, c * P:(c + 1) * P],
                                                   gkx[0:n, g, c, 64 * h:64 * h + 64], gvt[0:n, g, h, :], start=True, stop=True)
                    t["gla_updates"].made(ins)
                t["gla_masked"].next(pe)
                t["gla_states"].next(pe)
                for h, b in ((0, 6), (1, 2)):
                    r = slice(64 * h, 64 * h + 64)
                    for g, (g0, n) in enumerate(GROUPS):
                        nc.tensor.matmul(ps[:, b, g0:g0 + n], gvt[0:n, g, h, :], gatt[0:n, h, g0:g0 + n], start=True, stop=False, skip_group_check=True)
                        for c in range(n // C):
                            cc = g0 // C + c
                            slot = cc if cc < 8 else 9
                            ins = nc.tensor.matmul(ps[:, b, cc * C:(cc + 1) * C], gst[r, slot, :], gf[r, 2, cc * C:(cc + 1) * C],
                                                   start=False, stop=c == n // C - 1, skip_group_check=True)
                t["gla_o"].made(ins)
                t["gla_osq"].next(pe)
                nc.tensor.matmul(ps[:, 3, 0:T], K("ones"), go[:, 0, :], start=True, stop=True)
                t["gla_osum"].made(nc.tensor.matmul(ps[:, 4, 0:T], K("ones"), go[:, 1, :], start=True, stop=True))
                t["gla_read"].next(pe)
            leave(2, GLA_PER)

            with pe.Fori(0, 4) as i:
                enter(i, RW_PER, 3)
                for b in range(3):
                    if b == 2:
                        t["rw_evac"].wait(pe, 1)
                    s = take()
                    t["unit_used"].made(gemm(ps[:, b % 2, 0:T], s, 0, 128, hT))
                t["rw_evac"].k += 3
                t["rw_ksq"].next(pe)
                t["rw_ksum"].made(nc.tensor.matmul(ps[:, 2, 0:T], K("heads"), rt[:, 1, :], start=True, stop=True))
                t["rw_state_in"].next(pe)
                t["rw_state_turned"].made(nc.tensor.transpose(ps[:, 3, 0:P], rsi[:, :], K("ident")))
                t["rw_feats"].next(pe)
                for g, (g0, n) in enumerate(GROUPS):
                    for j, src in enumerate((rar[:, 0], rbk[:, 0], rbk[:, 1], rsh[:, 2])):
                        ins = nc.tensor.transpose(ps[0:n, 5 + g, j * P:(j + 1) * P], src[:, g0:g0 + n], K("ident"))
                    t["rw_turned"].made(ins)
                t["rw_evac"].wait(pe)
                for h in range(2):
                    r = slice(64 * h, 64 * h + 64)
                    for g, (g0, n) in enumerate(GROUPS):
                        ins = nc.tensor.matmul(ps[0:n, h, g0:g0 + n], rar[r, 0, g0:g0 + n], rbk[r, 0, g0:g0 + n], start=True, stop=True)
                t["rw_plain"].made(ins)
                t["rw_state_put"].next(pe)
                for g, (g0, n) in enumerate(GROUPS):
                    if g == 1:
                        t["rw_tok"].next(pe, 3)
                        t["rw_bkx"].next(pe, 3)
                    for h in range(2):
                        r = slice(64 * h, 64 * h + 64)
                        for j in range(2):
                            out = ps[0:n, 2 + 2 * g + h, 256 * j:256 * j + 256].rearrange("p (a t) -> p a t", a=2)[:, :, 0:n]
                            ins = nc.tensor.matmul(out, rbk[r, j, g0:g0 + n], rar[r, :, g0:g0 + n], start=True, stop=True)
                    t["rw_scores"].made(ins)
                t["rw_scored"].next(pe, 3)
                t["rw_q"].next(pe)

                def square(level, g, n, both):
                    for h in range(2):
                        if level == 0:
                            plain, turned = rpw[0:n, 0, g, h, 0, 0:n], rsc[0:n, g, h, 0, 0:n]
                        else:
                            plain, turned = (rpw[0:n, level % 2, g, h, x, 0:n] for x in range(2))
                        ins = nc.tensor.matmul(ps[0:n, 2 + g, 256 * h:256 * h + n], turned, plain, start=True, stop=True)
                        if both:
                            ins = nc.tensor.matmul(ps[0:n, 2 + g, 256 * h + 128:256 * h + 128 + n], plain, turned, start=True, stop=True)
                    t["rw_squared"].made(ins)

                for g, (g0, n) in enumerate(GROUPS):
                    square(0, g, n, True)
                for level in range(1, 5):
                    t["rw_power"].next(pe, 3)
                    if level > 1:
                        t["rw_grown"].next(pe, 3)
                    for g, (g0, n) in enumerate(GROUPS):
                        for h in range(2):
                            ins = nc.tensor.matmul(ps[0:n, 5 + g, P * h:P * h + n], rpw[0:n, level % 2, g, h, 0, 0:n],
                                                   rq[0:n, (level - 1) % 2, g, h, 0:n], start=True, stop=True)
                        t["rw_grow"].made(ins)
                        if level < 4:
                            square(level, g, n, level < 3)
                for g, (g0, n) in enumerate(GROUPS):
                    for h in range(2):
                        ins = nc.tensor.matmul(ps[0:n, 0, (2 * g + h) * 64:(2 * g + h + 1) * 64], rsc[0:n, g, h, 1, 0:n],
                                               rvt[0:n, g, 64 * h:64 * h + 64], start=True, stop=True)
                t["rw_akv"].made(ins)
                t["rw_x"].next(pe)
                t["rw_grown"].next(pe, 3)
                for g, (g0, n) in enumerate(GROUPS):
                    for h in range(2):
                        b, c0 = ((1, 0), (1, 256), (0, 0))[g]
                        ins = nc.tensor.matmul(ps[0:n, b, c0 + P * h:c0 + P * h + P], rq[0:n, 0, g, h, 0:n],
                                               rax[0:n, g, h, :, :], start=True, stop=True)
                t["rw_gh"].made(ins)
                t["rw_ghs"].next(pe)
                for g, (g0, n) in enumerate(GROUPS):
                    nch = n // C
                    for h in range(2):
                        r = slice(64 * h, 64 * h + 64)
                        nc.tensor.matmul(ps[r, 2 + g, 0:64 * nch], rgh[0:n, g, h, 0:64], rbx[0:n, g, 0:nch, r], start=True, stop=True)
                        for c in range(nch):
                            out = ps[r, 2 + g, 256 + 64 * c:320 + 64 * c]
                            nc.tensor.matmul(out, rbx[0:n, g, c, r], rgh[0:n, g, h, 64:128], start=True, stop=False)
                            ins = nc.tensor.matmul(out, rkx[0:n, g, c, r], rvt[0:n, g, r], start=False, stop=True)
                    t["rw_mn"].made(ins)
                for g, (g0, n) in enumerate(GROUPS):
                    for h in range(2):
                        r = slice(64 * h, 64 * h + 64)
                        ins = nc.tensor.matmul(ps[r, 5, g0:g0 + n], rgh[0:n, g, h, 0:64], rsc[0:n, g, h, 0, 128:128 + n], start=True, stop=True)
                t["rw_z"].made(ins)
                for g, (g0, n) in enumerate(GROUPS):
                    for h in range(2):
                        r = slice(64 * h, 64 * h + 64)
                        nc.tensor.matmul(ps[r, 6, g0:g0 + n], rgh[0:n, g, h, 64:128], rsc[0:n, g, h, 0, 128:128 + n], start=True, stop=False, skip_group_check=True)
                        ins = nc.tensor.matmul(ps[r, 6, g0:g0 + n], rvt[0:n, g, r], rsc[0:n, g, h, 1, 128:128 + n], start=False, stop=True, skip_group_check=True)
                t["rw_yi"].made(ins)
                t["rw_mns"].next(pe, 3)
                for c in (8, 1, 2, 3, 4, 5, 6, 7):
                    if c != 8:
                        t["rw_state"].next(pe, 2 if c == 2 else 1)
                    t["rw_step"].made(nc.tensor.matmul(ps[:, 2 if c == 8 else 0, 0:P], rmt[:, c, :], rst[:, c if c < 8 else 9, :], start=True, stop=True))
                t["rw_state"].next(pe)
                t["rw_zs"].next(pe)
                for c in range(NCH):
                    ins = nc.tensor.matmul(ps[:, 4, c * C:(c + 1) * C], rst[:, c if c < 8 else 9, :], rz[:, c * C:(c + 1) * C], start=True, stop=True)
                t["rw_ys"].made(ins)
                for s2, slot in enumerate((8, 10)):
                    ins = nc.tensor.transpose(ps[:, 2 + s2, 0:P], rst[:, slot, :], K("ident"))
                t["rw_final"].made(ins)
                t["rw_y"].next(pe)
                nc.tensor.matmul(ps[:, 0, 0:T], K("heads"), rt[:, 0, :], start=True, stop=True)
                t["rw_mean"].made(nc.tensor.matmul(ps[:, 5, 0:T], K("heads"), rt[:, 3, :], start=True, stop=True))
                t["rw_ysq"].next(pe)
                t["rw_var"].made(nc.tensor.matmul(ps[:, 1, 0:T], K("heads"), rt[:, 1, :], start=True, stop=True))
                t["rw_read"].next(pe)
            leave(4, RW_PER)
            t["shifts_turned"].made(nc.tensor.transpose(ps[0:28, 0, 0:P], shiftb[:, :, :].rearrange("p s j -> p (s j)"), K("ident")))
            t["mixed"].next(pe)
            for j in range(4):
                s = take()
                for c in range(2):
                    b = 2 * j + c
                    if b >= 4:
                        pe.wait_ge(sem["abo_added"], b - 3)
                    ins = gemm(ps[:, 1 + b % 4, 0:T], s, 128 * c, 256, yT)
                    t["unit_used" if c else "first_block"].made(ins)

            pe.wait_ge(sem["abo_added"], 8)
            norm()

            def ffn_up(first):
                for b in range(4):
                    if not first:
                        t["ffn_silu" if b < 2 else "ffn_made"].next(pe)
                    if b % 2 == 0:
                        s = take()
                    t["unit_used" if b % 2 else "first_block"].made(gemm(ps[:, b, 0:T], s, 128 * (b % 2), 256, hT))

            ffn_up(True)
            ffn_up(False)
            with pe.Fori(0, 3) as i:
                enter(i, FFN_PER, 6)
                for q in range(3):
                    ffn_up(False)
            leave(3, FFN_PER)

            def ffn_down(k, half, first, last):
                s = take()
                w = ring[:, s, 0:1024].rearrange("p (k n) -> p k n", k=2)
                for x in range(2):
                    for n in range(4):
                        ins = nc.tensor.matmul(ps[:, 4 - 4 * half + n, 0:T], w[:, x, n * P:(n + 1) * P], gT[:, k + x, :],
                                               start=first and x == 0, stop=last and x == 1)
                t["unit_used"].made(ins)
                return ins

            t["ffn_made"].next(pe, 2)
            for half in range(2):
                ffn_down(0, half, True, False)
                with pe.Fori(0, 3) as i:
                    enter(i, DOWN_PER, 3)
                    for q in range(3):
                        ffn_down(i * 6 + (2 + 2 * q), half, False, False)
                leave(3, DOWN_PER)
                ffn_down(20, half, False, True)
            pe.wait_ge(sem["ffn_added"], 8)
            norm()
            with pe.Fori(0, 4) as i:
                enter(i, RET_PER, 6)
                for b in range(12):
                    if b == 0:
                        t["ret_done"].wait(pe, 1)
                    if b >= 4:
                        t["ret_evac"].wait(pe, b - 3)
                    if b % 2 == 0:
                        s = take()
                    t["unit_used" if b % 2 else "first_block"].made(gemm(ps[:, b % 4, 0:T], s, 128 * (b % 2), 256, hT))
                t["ret_evac"].next(pe, 12)
                for g, (g0, n) in enumerate(GROUPS):
                    for j in range(4):
                        ins = nc.tensor.transpose(ps[0:n, 4 + g, j * P:(j + 1) * P], rvf[:, j, g0:g0 + n], K("ident"))
                t["ret_vturned"].made(ins)
                t["ret_rotated"].next(pe)
                for g, (g0, n) in enumerate(GROUPS):
                    for j in range(2):
                        ins = nc.tensor.transpose(ps[0:n, g // 2, (2 * (g % 2) + j) * P:(2 * (g % 2) + j + 1) * P], rrot[:, 2 + j, g0:g0 + n], K("ident"))
                t["ret_kturned"].made(ins)
                for out, ks, qs in ((ps[:, 2, 0:256], slice(0, 128), slice(0, 256)), (ps[:, 3, 0:128], slice(128, 256), slice(128, 256)),
                                    (ps[0:TS, 3, 128:160], slice(TP, T), slice(TP, T))):
                    for j in range(2):
                        ins = nc.tensor.matmul(out, rrot[:, 2 + j, ks], rrot[:, j, qs], start=j == 0, stop=j == 1)
                t["ret_scores"].made(ins)
                t["ret_vtok"].next(pe)
                t["ret_ktok"].next(pe)
                t["ret_att"].next(pe)
                t["ret_state_in"].next(pe, 16)
                for j in range(4):
                    c = slice(j * P, (j + 1) * P)
                    nc.tensor.matmul(ps[:, 4 + j, 0:256], rV[:, 0, c], ratt[:, 0:256], start=True, stop=False, skip_group_check=True)
                    nc.tensor.matmul(ps[:, 4 + j, 128:256], rV[:, 1, c], ratt[:, 256:384], start=False, stop=True, skip_group_check=True)
                    nc.tensor.matmul(ps[:, 4 + j, 256:T], rV[0:TS, 2, c], ratt[0:TS, 384:416], start=True, stop=False, skip_group_check=True)
                    for x in range(2):
                        ins = nc.tensor.matmul(ps[:, 4 + j, 256:T], rS0[:, x, c], rqs[:, x, :], start=False, stop=x == 1, skip_group_check=True)
                t["ret_o"].made(ins)
                for x in range(2):
                    c = slice(x * P, (x + 1) * P)
                    nc.tensor.matmul(ps[:, x, :], rK[:, 0, c], rV[:, 0, :], start=True, stop=False)
                    nc.tensor.matmul(ps[:, x, :], rK[:, 1, c], rV[:, 1, :], start=False, stop=True)
                    ins = nc.tensor.matmul(ps[:, 2 + x, :], rK[0:TS, 2, c], rV[0:TS, 2, :], start=True, stop=True)
                t["ret_states"].made(ins)
                t["ret_stated_p"].next(pe)
                t["ret_stated_s"].next(pe)
                t["ret_osb"].next(pe)
                for j in range(4):
                    ins = nc.tensor.matmul(ps[:, 0, 0:T], K("ones"), ro[:, j, :], start=j == 0, stop=j == 3)
                t["ret_mean"].made(ins)
                t["ret_osq"].next(pe)
                for j in range(4):
                    ins = nc.tensor.matmul(ps[:, 1, 0:T], K("ones"), rosq[:, j, :], start=j == 0, stop=j == 3)
                t["ret_var"].made(ins)
                t["ret_done"].k += 1
            leave(4, RET_PER)
            t["ret_done"].wait(pe, 1)
            for j in range(4):
                for kh in range(2):
                    s = take()
                    for c in range(2):
                        b = 2 * j + c
                        if b >= 4 and kh == 0:
                            pe.wait_ge(sem["reto_added"], b - 3)
                        ins = gemm(ps[:, 3 + b % 4, 0:T], s, 128 * c, 256, yR[:, KD * kh:KD * kh + KD, :], start=kh == 0, stop=kh == 1)
                        t["unit_used" if c else "first_block"].made(ins)
            pe.wait_ge(sem["reto_added"], 8)
            norm()
            for g, (g0, n) in enumerate(GROUPS):
                for k in range(KD):
                    ins = nc.tensor.matmul(ps[0:n, 0, 8 * g:8 * g + 8], hT[:, k, g0:g0 + n], w_router[:, k, :], start=k == 0, stop=k == KD - 1)
                if g == 0:
                    t["slot_free"].made(ins, RINGX)
            t["logits"].made(ins)
            for g, (g0, n) in enumerate(GROUPS):
                for k in range(KD):
                    ins = nc.tensor.transpose(ps[0:n, 1 + 2 * g + k // 4, (k % 4) * P:(k % 4 + 1) * P], hT[:, k, g0:g0 + n], K("ident"))
            t["frames_turned"].made(ins)
            t["picked"].next(pe)
            for g, (g0, n) in enumerate(GROUPS):
                for g2 in range(g):
                    nc.tensor.matmul(ps[0:n, 7, 8 * g:8 * g + 8], K("ones", 0, n), pick[:, g2, 0:NEXP], start=g2 == 0, stop=False)
                nc.tensor.matmul(ps[0:n, 7, 8 * g:8 * g + 8], K("before", 0, n)[0:n], pick[0:n, g, 0:NEXP], start=g == 0, stop=True)
            for g, (g0, n) in enumerate(GROUPS):
                ins = nc.tensor.matmul(ps[:, 7, 32:40], K("ones")[0:n], pick[0:n, g, 0:NEXP], start=g == 0, stop=g == 2)
            t["placed"].made(ins)
            pe.wait_ge(sem["rounds_known"], 1)
            pe.wait_ge(sem["frames_tok"], 1)
            def gather():
                for k in range(KD):
                    for g, (g0, n) in enumerate(GROUPS):
                        ins = nc.tensor.matmul(ps[:, 4 + k // 4, (k % 4) * CAP:(k % 4 + 1) * CAP], htok[0:n, g, k * P:(k + 1) * P], take_f[0:n, g, :], start=g == 0, stop=g == 2)
                t["x_taken"].made(ins)

            def scatter(k):
                if k >= 2:
                    t["x_added"].next(pe)
                t["x_out"].made(nc.tensor.matmul(ps[:, 4 + k % 2, 0:T], yx[:, k * P:(k + 1) * P], giveT[:, :], start=True, stop=True))

            t["x_give"].next(pe)
            gather()
            n_rounds = count_rounds(pe)
            with pe.Fori(0, n_rounds) as r:
                with pe.Fori(0, NEXP) as e:
                    turn = r * NEXP + e
                    enter(turn, X_PER, 33)

                    def x_take(k):
                        pe.wait_ge(x_arrived[k % RINGX], turn * 48 + 16 * (k // RINGX + 1))
                        return k % RINGX

                    t["x_h"].next(pe)
                    for j in range(KF // 2):
                        for x in range(2):
                            s = x_take(2 * j + x)
                            w = xring[:, s, :].rearrange("p (k n) -> p k n", k=KD)
                            if x == 0 and j >= 2:
                                t["x_read"].next(pe)
                            for c in range(2):
                                for k in range(KD):
                                    ins = nc.tensor.matmul(ps[:, 2 * (j % 2) + x, c * CAP:(c + 1) * CAP], w[:, k, c * P:(c + 1) * P], hx[:, k, :], start=k == 0, stop=k == KD - 1)
                            t["slot_free"].made(ins)
                        if j == 1:
                            t["x_y"].next(pe)
                        if 1 <= j <= 4:
                            scatter(2 * j - 2)
                            scatter(2 * j - 1)
                    t["x_added"].next(pe, 2)
                    t["x_read"].next(pe)
                    t["x_give"].next(pe)
                    for g, (g0, n) in enumerate(GROUPS):
                        ins = nc.tensor.transpose(ps[0:CAP, 2, g0:g0 + n], give_f[0:n, g, :], K("ident", 0, n)[0:n])
                    gather()
                    for j in range(KF // 2):
                        s = x_take(22 + j)
                        w = xring[:, s, :].rearrange("p (k n) -> p k n", k=2)
                        if j == 0:
                            t["x_read"].next(pe)
                        for x in range(2):
                            for c in range(2):
                                ins = nc.tensor.matmul(ps[0:CAP, 6 + c, :], gx_[:, 2 * j + x, :], w[:, x, 512 * c:512 * c + 512], start=j == 0 and x == 0, stop=j == 10 and x == 1)
                        t["slot_free"].made(ins)
            for name in X_PER:
                t[name].k = 0
            enter(n_rounds * NEXP, X_PER, 33)
            t["x_h"].next(pe)
            t["x_y"].next(pe)
            for k in range(KD):
                scatter(k)
            t["x_added"].next(pe, 2)
            pe.wait_ge(sem["x_ready"], 4)
            norm()
            for g, (g0, n) in enumerate(GROUPS):
                for k in range(KD):
                    ins = nc.tensor.transpose(ps[0:n, 1 + 2 * g + k // 4, (k % 4) * P:(k % 4 + 1) * P], hT[:, k, g0:g0 + n], K("ident"))
                t["y_turned"].made(ins)

        @block.scalar
        def _(act):
            t = {n: Tally(s, n) for n, s in sem.items()}
            A = nc.scalar.activation

            def enter(i, per):
                for n, p in per.items():
                    t[n].enter(i, p)

            def leave(n, per):
                for name in per:
                    t[name].leave(n)

            def norm(r):
                t["x_ready"].next(act)
                t["squares"].made(A(yT[:, :, :], xT[:, :, :], ACT.Square))
                t["square_sums"].next(act)
                t["roots"].made(A(rstd[:, 0, :], ps[:, 7, 0:T], ACT.Sqrt, bias=eps(EPS), scale=1.0 / D))

            for n, (name, _w) in enumerate(ROWS):
                at, w = VEC[name]
                src = a[name]
                while len(src.shape) > 2:
                    src = src[0]
                if len(src.shape) == 2:
                    src = src.rearrange("a n -> (a n)") if src.shape[0] > 1 and name != "rwkv_r_k" else (src.rearrange("a n -> (a n)"))
                act.dma_start(rows[at % P:at % P + w, at // P, :], src.rearrange("(j p) -> j p", p=P)).then_inc(sem["in_rows"], 16)
            act.dma_start(const[:, :], a["const"]).then_inc(sem["in_const"], 16)
            for g in range(2):
                act.dma_start(xrow[:, g, :], a["x_prompt"][0, g * P:(g + 1) * P, :]).then_inc(sem["in_x"], 16)
            act.dma_start(xrow[0:TS, 2, :], a["x_sample"][0]).then_inc(sem["in_x"], 16)
            act.dma_start(w_ga[:, :, :], W_IN[:, :, GA:GA + 16]).then_inc(sem["in_lora"], 16)
            act.dma_start(w_gate[:, :], a["gla_w_gate2"][0]).then_inc(sem["in_lora"], 16)
            act.dma_start(w_wa[0:64, :], a["rwkv_w2"][0]).then_inc(sem["in_lora"], 16)
            act.dma_start(w_wa[64:128, :], a["rwkv_a2"][0]).then_inc(sem["in_lora"], 16)
            act.dma_start(w_g[:, :], a["rwkv_g2"][0]).then_inc(sem["in_lora"], 16)
            act.dma_start(w_router[:, :, :], a["moe_router"][0].rearrange("(k p) e -> p k e", p=P)).then_inc(sem["in_lora"], 16)
            act.dma_start(gla_in[:, :, :], a["state_gla"][0, 0].rearrange("(q h) k v -> (h k) q v", q=2)).then_inc(sem["in_lora"], 16)
            act.dma_start(rw_in[:, :, :], a["state_rwkv"][0, 0].rearrange("(q h) v k -> (h v) q k", q=4)).then_inc(sem["in_lora"], 16)

            act.wait_ge(sem["eps_set"], 1)
            for k in range(KD):
                t["x_turned"].next(act)
                ins = A(xT[:, k, :], ps[:, 2 + k % 4, 0:T], ACT.Copy)
                t["x_copied"].made(ins)
            act.wait_ge(sem["x_copied"], KD)
            t["squares"].made(A(yT[:, :, :], xT[:, :, :], ACT.Square))
            t["square_sums"].next(act)
            t["roots"].made(A(rstd[:, 0, :], ps[:, 7, 0:T], ACT.Sqrt, bias=eps(EPS), scale=1.0 / D))

            t["first_block"].next(act)
            t["unit_used"].next(act)
            A(lora[:, 0:2, :], ps[:, 0:2, 0:T], ACT.Copy)
            t["lora_raw"].made(A(lora[:, 2:4, 1:T], ps[:, 0:2, 0:T - 1], ACT.Copy))
            t["ga_block"].next(act)
            t["gate_in"].made(A(gaT[:, :], ps[0:16, 2, 0:T], ACT.Copy))
            t["lora_shifted"].next(act)
            A(lora[0:64, 4, :], lora[0:64, 4, :], ACT.Tanh)
            t["lora_in"].made(A(lora[:, 5, :], lora[:, 5, :], ACT.Sigmoid))
            for j in range(4):
                t["lora_mixed"].next(act)
                b = 3 * (j % 2)
                if j == 1:
                    act.wait_ge(sem["gate_out"], 1)
                A(lw[:, j, :], ps[:, b, 0:T], ACT.Sigmoid, bias=V("rwkv_w0", j))
                A(av[:, j, :], ps[:, b + 1, 0:T], ACT.Sigmoid, bias=V("rwkv_a0", j))
                t["lora_out"].made(A(gv[:, j, :], ps[:, b + 2, 0:T], ACT.Copy))
            t["gate_out"].next(act)
            t["act_chain"].link(act, A(gz[:, 1], gz[:, 0], ACT.Abs))
            t["act_chain"].link(act, A(gz[:, 1], gz[:, 1], ACT.Exp, scale=-1.0))
            t["gate_log"].made(A(gz[:, 1], gz[:, 1], ACT.Ln, bias=one()))
            t["gate_sums"].next(act)
            A(gexp[:, 0], gz[:, 1], ACT.Exp)
            A(gexp[:, 1], gz[:, 1], ACT.Exp, scale=-1.0)
            A(gexp[:, 2], gz[:, 0], ACT.Exp)
            A(gexp[:, 3], gz[:, 2], ACT.Exp)
            t["gate_exps"].made(A(gend[:, :, :], gz[:, 0].rearrange("p q (c t) -> p q c t", t=C)[:, :, :, C - 1], ACT.Exp))
            t["decay_sums"].next(act)
            A(rexp[:, 0], lw[:, :, :], ACT.Exp)
            A(rexp[:, 2], lw[:, :, :], ACT.Exp, scale=-1.0)
            t["decay_exps"].made(A(rexp[:, 1], rexp[:, 1], ACT.Exp))

            with act.Fori(0, 2) as i:
                enter(i, GLA_PER)
                for b in range(6):
                    t["unit_used"].next(act)
                    if b == 0 or b == 2 or b == 4:
                        pass
                    ins = A(gx[:, b, :], ps[:, b % 2, 0:T], ACT.Copy, scale=0.125 if b == 0 else 1.0)
                    t["gla_evac"].made(ins)
                t["gla_evac"].wait(act)
                t["gla_og"].made(A(go[:, 2:4, :], gx[:, 4:6, :], ACT.Sigmoid))
                for g, (g0, n) in enumerate(GROUPS):
                    t["gla_turned"].next(act)
                    t["gla_kx"].next(act)
                    t["gla_vt"].made(A(gvt[0:n, g, :, :], ps[0:n, 4 + g, P:3 * P].rearrange("p (h v) -> p h v", h=2), ACT.Copy))
                t["gla_o"].next(act)
                A(go[:, 0, :], ps[:, 6, 0:T], ACT.Square)
                t["gla_osq"].made(A(go[:, 1, :], ps[:, 2, 0:T], ACT.Square))
                t["gla_osum"].next(act)
                t["gla_root"].made(A(go[:, 0:2, :], ps[:, 3:5, 0:T], ACT.Sqrt, bias=eps(EPS), scale=1.0 / P))
                t["gla_read"].next(act)
            leave(2, GLA_PER)

            with act.Fori(0, 4) as i:
                enter(i, RW_PER)
                for b in range(3):
                    t["unit_used"].next(act)
                    A(rx[:, b, :], ps[:, b % 2, 0:T], ACT.Copy)
                    t["rw_evac"].made(A(rp[:, b, 1:T], ps[:, b % 2, 0:T - 1], ACT.Copy))
                t["rw_ksum"].next(act)
                t["rw_kroot"].made(A(rt[:, 2, :], ps[:, 2, 0:T], ACT.Sqrt))
                t["rw_state_turned"].next(act)
                t["rw_state_put"].made(A(rst[:, 9, :], ps[:, 3, 0:P], ACT.Copy))
                for g, (g0, n) in enumerate(GROUPS):
                    t["rw_turned"].next(act)
                    t["rw_bkx"].next(act)
                    A(rax[0:n, g, :, 0, :], ps[0:n, 5 + g, 0:P].rearrange("p (h k) -> p h k", h=2), ACT.Copy)
                    t["rw_tok"].made(A(rvt[0:n, g, :], ps[0:n, 5 + g, 3 * P:4 * P], ACT.Copy))
                for level in range(1, 5):
                    for g, (g0, n) in enumerate(GROUPS):
                        t["rw_squared"].next(act)
                        src = ps[0:n, 2 + g, :].rearrange("p (h a t) -> p h a t", h=2, a=2)
                        x = 2 if level < 4 else 1
                        for h in range(2):
                            ins = A(rpw[0:n, level % 2, g, h, 0:x, 0:n], src[:, h, 0:x, 0:n], ACT.Copy)
                        t["rw_power"].made(ins)
                t["rw_akv"].next(act)
                A(rax[:, 0:2, :, 1, :], ps[:, 0, 0:256].rearrange("p (g h v) -> p g h v", g=2, h=2), ACT.Copy)
                t["rw_x"].made(A(rax[0:TS, 2, :, 1, :], ps[0:TS, 0, 256:384].rearrange("p (h v) -> p h v", h=2), ACT.Copy))
                t["rw_gh"].next(act)
                A(rgh[:, 0:2, :, :], ps[:, 1, :].rearrange("p (g h v) -> p g h v", g=2, h=2), ACT.Copy)
                t["rw_ghs"].made(A(rgh[0:TS, 2, :, :], ps[0:TS, 0, 0:256].rearrange("p (h v) -> p h v", h=2), ACT.Copy))
                t["rw_yi"].next(act)
                t["rw_yis"].made(A(ryi[:, :], ps[:, 6, 0:T], ACT.Copy))
                t["rw_final"].next(act)
                A(rw_out[0:64, i, :, :], ps[0:64, 2:4, 0:64], ACT.Copy)
                t["rw_out"].made(A(rw_out[64:128, i, :, :], ps[64:128, 2:4, 64:P], ACT.Copy))
                t["rw_centred"].next(act)
                t["rw_ysq"].made(A(rt[:, 1, :], rt[:, 0, :], ACT.Square))
                t["rw_var"].next(act)
                t["rw_root"].made(A(rt[:, 2, :], ps[:, 1, 0:T], ACT.Sqrt, bias=eps(64e-5), scale=1.0 / 64))
                t["rw_read"].next(act)
            leave(4, RW_PER)
            t["shifts_turned"].next(act)
            t["shifts_out"].made(A(shifto[:, :], ps[0:28, 0, 0:P], ACT.Copy))

            act.wait_ge(sem["abo_added"], 8)
            norm(1)
            t["first_block"].k += 4
            t["unit_used"].k += 4

            def ffn_up(first):
                for b in range(2):
                    t["unit_used" if b else "first_block"].next(act)
                    if not first:
                        t["ffn_made"].next(act)
                    t["ffn_silu"].made(A(fsil[:, b, :], ps[:, b, 0:T], ACT.Silu))
                t["unit_used"].k += 1
                t["first_block"].k += 1

            ffn_up(True)
            ffn_up(False)
            with act.Fori(0, 3) as i:
                enter(i, FFN_PER)
                for q in range(3):
                    ffn_up(False)
            leave(3, FFN_PER)
            act.wait_ge(sem["ffn_added"], 8)
            norm(2)
            t["unit_used"].k += 22
            with act.Fori(0, 4) as i:
                enter(i, RET_PER)
                t["ret_done"].wait(act, 1)
                for b in range(12):
                    t["unit_used" if b % 2 else "first_block"].next(act)
                    dst = (rqk, rvf, rgf)[b // 4][:, b % 4, :]
                    t["ret_evac"].made(A(dst, ps[:, b % 4, 0:T], ACT.Silu if b >= 8 else ACT.Copy))
                t["ret_vturned"].next(act)
                A(rV[:, 0:2, :], ps[:, 4:6, :], ACT.Copy)
                t["ret_vtok"].made(A(rV[0:TS, 2, :], ps[0:TS, 6, :], ACT.Copy))
                t["ret_o"].next(act)
                t["ret_osb"].made(A(ro[:, :, :], ps[:, 4:8, 0:T], ACT.Copy))
                t["ret_states"].next(act)
                t["ret_buffer"].next(act)
                t["ret_stated_p"].made(A(rS[:, 0, :, :], ps[:, 0:2, :], ACT.Copy))
                t["ret_centred"].next(act)
                t["ret_osq"].made(A(rosq[:, :, :], ro[:, :, :], ACT.Square))
                t["ret_var"].next(act)
                t["ret_root"].made(A(rstd[:, 0, :], ps[:, 1, 0:T], ACT.Sqrt, bias=eps(1e-5), scale=1.0 / 512))
                t["ret_done"].k += 1
            leave(4, RET_PER)
            act.wait_ge(sem["reto_added"], 8)
            norm(3)
            act.wait_ge(sem["ret_stored"], 32 * 4)
            t["logits_centred"].next(act)
            for g, (g0, n) in enumerate(GROUPS):
                ins = A(prob[0:n, g, :], prob[0:n, g, :], ACT.Exp)
            t["logits_exp"].made(ins)
            t["frames_turned"].next(act)
            for g, (g0, n) in enumerate(GROUPS):
                ins = A(htok[0:n, g, :], ps[0:n, 1 + 2 * g:3 + 2 * g, :].rearrange("p a n -> p (a n)"), ACT.Copy)
            t["frames_tok"].made(ins)
            act.wait_ge(sem["rounds_known"], 1)
            t["slot_free"].k = RINGX
            def keep_frames():
                for x in range(2):
                    ins = A(hx[:, 4 * x:4 * x + 4, :], ps[:, 4 + x, 0:4 * CAP].rearrange("p (k n) -> p k n", k=4), ACT.Copy)
                t["x_h"].made(ins)

            t["x_taken"].next(act)
            keep_frames()
            with act.Fori(0, count_rounds(act)) as r:
                with act.Fori(0, NEXP) as e:
                    enter(r * NEXP + e, X_PER)
                    for j in range(KF // 2):
                        t["slot_free"].next(act)
                        if j >= 2:
                            t["x_read"].next(act)
                        t["x_silu"].made(A(xsil[:, j % 2, :], ps[:, 2 * (j % 2), 0:2 * CAP], ACT.Silu))
                        t["slot_free"].k += 1
                    t["x_read"].k += 2
                    t["x_taken"].next(act)
                    A(giveT[:, :], ps[0:CAP, 2, 0:T], ACT.Copy)
                    keep_frames()
                    t["slot_free"].next(act, 11)
                    A(yx[:, 0:512], ps[0:CAP, 6, :], ACT.Copy)
                    t["x_y"].made(A(yx[:, 512:D], ps[0:CAP, 7, :], ACT.Copy))
            norm(4)
            for g, (g0, n) in enumerate(GROUPS):
                t["y_turned"].next(act)
                ins = A(ytok[0:n, g, :], ps[0:n, 1 + 2 * g:3 + 2 * g, :].rearrange("p a n -> p (a n)"), ACT.Copy)
                t["y_copied"].made(ins)
                act.wait_ge(sem["y_copied"], g + 1)
                act.dma_start(o[0][0, g0:g0 + n, :] if g < 2 else o[1][0], ytok[0:n, g, :]).then_inc(sem["y_stored"], 16)
            act.wait_ge(sem["y_stored"], 16 * 3)

        @block.vector
        def _(dve):
            t = {n: Tally(s, n) for n, s in sem.items()}
            v = nc.vector

            def enter(i, per):
                for n, p in per.items():
                    t[n].enter(i, p)

            def leave(n, per):
                for name in per:
                    t[name].leave(n)

            def link(ins):
                t["dve_chain"].link(dve, ins)

            def tt(out, x, y, op=ALU.mult):
                return v.tensor_tensor(out, x, y, op)

            def stt(out, x, s, y, op0, op1):
                return v.scalar_tensor_tensor(out=out, in0=x, scalar=s, in1=y, op0=op0, op1=op1)

            def norm(r):
                t["roots"].next(dve)
                link(v.reciprocal(rstd[:, 1, :], rstd[:, 0, :]))
                w = norm_columns(r)
                for k in range(KD):
                    ins = stt(hT[:, k, :], xT[:, k, :], w[:, k:k + 1], rstd[:, 1, :], ALU.mult, ALU.mult)
                t["normed"].made(ins)

            v.memset(epsb[:, 0:1], EPS)
            v.memset(epsb[:, 1:2], 64e-5)
            v.memset(epsb[:, 2:3], 1.0)
            t["eps_set"].made(v.memset(epsb[:, 3:4], 1e-5))
            v.memset(gst[:, 0, :], 0.0)
            link(v.memset(lora[:, 2:4, 0:1], 0.0))
            t["vec_turned"].next(dve)
            v.tensor_copy(vec[:, 0:99], ps[:, 0, 0:99])
            link(v.tensor_copy(vec[:, P:P + 32], ps[:, 1, 0:32]))
            v.tensor_scalar(omka[:, :], V("rwkv_k_a", 0, 4), -1.0, 1.0, ALU.mult, ALU.add)
            norm(0)

            t["lora_raw"].next(dve)
            for j in range(2):
                v.tensor_copy(lora[:, 2 + j, TP:TP + 1], V("state_shift", 12 + j))
            for s2, col in enumerate((TP - 1, T - 1)):
                ins = v.tensor_copy(shiftb[:, s2, 12:14], lora[:, 0:2, col])
            link(ins)
            link(tt(lora[:, 2:4, :], lora[:, 2:4, :], lora[:, 0:2, :], ALU.subtract))
            for j in range(2):
                ins = stt(lora[:, 4 + j, :], lora[:, 2 + j, :], V("rwkv_mu", 12 + j), lora[:, j, :], ALU.mult, ALU.add)
            t["lora_shifted"].made(ins)
            t["gate_blocks"].next(dve)
            for j in range(2):
                ins = v.tensor_scalar(gz[:, 0, j, :], ps[:, 3 + j, 0:T], V("gla_b_gate", j), None, ALU.add)
            t["gate_out"].made(ins)
            t["gate_out"].wait(dve)
            link(v.tensor_scalar(gz[:, 2], gz[:, 0], 0.0, None, ALU.min))
            t["gate_log"].next(dve)
            link(tt(gz[:, 2], gz[:, 2], gz[:, 1], ALU.subtract))
            link(v.tensor_scalar(gz[:, 2], gz[:, 2], 1.0 / 16, None, ALU.mult))
            for j in range(2):
                ins = v.tensor_tensor_scan(gz[:, 0, j, :], K("scan"), gz[:, 2, j, :], 0.0, ALU.mult, ALU.add)
            link(ins)
            for j in range(2):
                b = chunks(gz[:, 0, j, :])
                last = b[:, :, C - 1:C].to_broadcast([P, NCH, C])
                stt(chunks(gz[:, 1, j, :]), last, -0.5, b, ALU.mult, ALU.add)
                ins = tt(chunks(gz[:, 2, j, :]), last, b, ALU.subtract)
            t["gate_sums"].made(ins)
            t["lora_out"].next(dve, 4)
            link(v.tensor_scalar(rexp[:, 0], lw[:, :, :], -float(np.exp(-0.5)), None, ALU.mult))
            for j in range(4):
                ins = v.tensor_tensor_scan(lw[:, j, :], K("scan"), rexp[:, 0, j, :], 0.0, ALU.mult, ALU.add)
            link(ins)
            link(tt(rexp[:, 1], lw[:, :, :], rexp[:, 0], ALU.subtract))
            t["decay_sums"].made(v.memset(epsb[:, 4:5], 0.0))

            t["gate_exps"].next(dve)
            dve.wait_ge(sem["in_lora"], 16 * SMALL_LOADS)
            with dve.Fori(0, 2) as i:
                enter(i, GLA_PER)
                t["gla_evac"].k += 1
                t["gla_evac"].next(dve)
                tt(gf[:, 0, :], gx[:, 0, :], gexp[:, 0, i, :])
                tt(gf[:, 1, :], gx[:, 1, :], gexp[:, 1, i, :])
                tt(gf[:, 2, :], gx[:, 0, :], gexp[:, 2, i, :])
                t["gla_feats"].made(tt(gf[:, 3, :], gx[:, 1, :], gexp[:, 3, i, :]))
                v.tensor_copy(gst[:, 9, :], gla_in[:, i, :])
                t["gla_scores"].next(dve)
                tt(gatt[:, :, 0:256], ps[:, 2:4, 0:256], K("incl_t").unsqueeze(1).to_broadcast([P, 2, 256]))
                t["gla_masked"].made(tt(gatt[0:TS, :, 256:T], ps[0:TS, 2:4, 256:T], K("incl_t", 0, TS)[0:TS].unsqueeze(1).to_broadcast([TS, 2, TS])))
                for g, (g0, n) in enumerate(GROUPS):
                    t["gla_turned"].next(dve)
                    nch = n // C
                    t["gla_kx"].made(tt(gkx[0:n, g, 0:nch, :], ps[0:n, 4 + g, 0:P].unsqueeze(1).to_broadcast([n, nch, P]),
                                        K("chunk", 0, nch)[0:n].unsqueeze(2).to_broadcast([n, nch, P])))
                for g, b in ((0, 7), (1, 4), (2, 5)):
                    t["gla_updates"].next(dve)
                    for c in range(GROUPS[g][1] // C):
                        cc = 4 * g + c
                        src, dst = (cc, cc + 1) if cc < 8 else (9, 10)
                        link(stt(gst[:, dst, :], gst[:, src, :], gend[:, i, cc:cc + 1], ps[:, b, c * P:(c + 1) * P], ALU.mult, ALU.add))
                v.tensor_copy(gla_out[:, i, 0, :], gst[:, 8, :])
                t["gla_states"].made(v.tensor_copy(gla_out[:, i, 1, :], gst[:, 10, :]))
                t["gla_evac"].next(dve, 4)
                t["gla_og"].next(dve)
                link(tt(go[:, 2:4, :], go[:, 2:4, :], gx[:, 4:6, :]))
                t["gla_root"].next(dve)
                link(v.reciprocal(gf[:, 0:2, :], go[:, 0:2, :]))
                for h, b in ((0, 6), (1, 2)):
                    ins = stt(gf[:, 2 + h, :], ps[:, b, 0:T], V("gla_norm"), gf[:, h, :], ALU.mult, ALU.mult)
                link(ins)
                t["gla_read"].made(tt(yT[:, bass.ds(i * 2, 2), :], gf[:, 2:4, :], go[:, 2:4, :]))
            leave(2, GLA_PER)

            t["decay_exps"].next(dve)
            v.memset(rst[:, 0, :], 0.0)
            v.memset(rsi[:, :], 0.0)
            v.memset(rmt[:, :, :], 0.0)
            link(v.memset(rnw[:, :, :], 0.0))
            with dve.Fori(0, 4) as i:
                enter(i, RW_PER)
                v.tensor_copy(rsi[0:64, 0:64], rw_in[0:64, i, :])
                t["rw_state_in"].made(v.tensor_copy(rsi[64:128, 64:128], rw_in[64:128, i, :]))
                t["rw_evac"].next(dve, 3)
                v.memset(rp[:, :, 0:1], 0.0)
                for b in range(3):
                    v.tensor_copy(rp[:, b, TP:TP + 1], vec[:, bass.ds(i + (VEC["state_shift"][0] + 4 * b), 1)])
                    v.tensor_copy(shiftb[:, 0, bass.ds(i + 4 * b, 1)], rx[:, b, TP - 1:TP])
                    ins = v.tensor_copy(shiftb[:, 1, bass.ds(i + 4 * b, 1)], rx[:, b, T - 1:T])
                link(ins)
                link(tt(rp[:, :, :], rp[:, :, :], rx[:, :, :], ALU.subtract))
                for b in range(3):
                    ins = stt(rsh[:, b, :], rp[:, b, :], vec[:, bass.ds(i + (VEC["rwkv_mu"][0] + 4 * b), 1)], rx[:, b, :], ALU.mult, ALU.add)
                link(ins)
                link(v.tensor_scalar(rt[:, 0, :], rsh[:, 1, :], vec[:, bass.ds(i + VEC["rwkv_k_k"][0], 1)], None, ALU.mult))
                t["rw_ksq"].made(tt(rt[:, 1, :], rt[:, 0, :], rt[:, 0, :]))
                link(v.tensor_scalar(rt[:, 4, :], av[:, i, :], vec[:, bass.ds(i + VEC["rwkv_k_a"][0], 1)], omka[:, bass.ds(i, 1)], ALU.mult, ALU.add))
                link(tt(rkn[:, :], rt[:, 4, :], rsh[:, 1, :]))
                tt(rar[:, 1, :], rsh[:, 0, :], rexp[:, 0, i, :])
                tt(rbk[:, 1, :], rkn[:, :], rexp[:, 2, i, :])
                t["rw_kroot"].next(dve)
                link(v.tensor_scalar(rt[:, 2, :], rt[:, 2, :], 1e-12, None, ALU.max))
                link(v.reciprocal(rt[:, 3, :], rt[:, 2, :]))
                link(tt(rkk[:, :], rt[:, 0, :], rt[:, 3, :]))
                stt(rar[:, 0, :], rkk[:, :], -1.0, rexp[:, 1, i, :], ALU.mult, ALU.mult)
                link(tt(rt[:, 2, :], rkk[:, :], av[:, i, :]))
                t["rw_feats"].made(tt(rbk[:, 0, :], rt[:, 2, :], rexp[:, 2, i, :]))
                for g, (g0, n) in enumerate(GROUPS):
                    nch = n // C
                    t["rw_turned"].next(dve)
                    for j, dst in enumerate((rbx, rkx)):
                        ins = tt(dst[0:n, g, 0:nch, :], ps[0:n, 5 + g, (1 + j) * P:(2 + j) * P].unsqueeze(1).to_broadcast([n, nch, P]),
                                 K("chunk", 0, nch)[0:n].unsqueeze(2).to_broadcast([n, nch, P]))
                    t["rw_bkx"].made(ins)
                t["rw_plain"].next(dve)
                for h in range(2):
                    for g, (g0, n) in enumerate(GROUPS):
                        tt(rpw[0:n, 0, g, h, 0, 0:n], ps[0:n, h, g0:g0 + n], K("strict", 0, n)[0:n])
                for g, (g0, n) in enumerate(GROUPS):
                    t["rw_scores"].next(dve)
                    mask = K("strict_incl_t")[0:n].rearrange("p (a t) -> p a t", a=2)[:, :, 0:n]
                    for h in range(2):
                        src = ps[0:n, 2 + 2 * g + h, :].rearrange("p (b a t) -> p b a t", b=2, a=2)[:, :, :, 0:n]
                        dst = rsc[0:n, g, h, :, :].rearrange("p b (a t) -> p b a t", a=2)[:, :, :, 0:n]
                        for b in range(2):
                            ins = tt(dst[:, b], src[:, b], mask)
                    t["rw_scored"].made(ins)
                t["rw_scored"].wait(dve)
                for g, (g0, n) in enumerate(GROUPS):
                    ins = tt(rq[0:n, 0, g, :, 0:n], rsc[0:n, g, :, 0, 0:n], K("ident", 0, n)[0:n].unsqueeze(1).to_broadcast([n, 2, n]), ALU.add)
                t["rw_q"].made(ins)
                t["rw_q"].wait(dve)
                for level in range(1, 5):
                    for g, (g0, n) in enumerate(GROUPS):
                        t["rw_grow"].next(dve)
                        src = ps[0:n, 5 + g, 0:256].rearrange("p (h t) -> p h t", h=2)[:, :, 0:n]
                        t["rw_grown"].made(tt(rq[0:n, level % 2, g, :, 0:n], src, rq[0:n, (level - 1) % 2, g, :, 0:n], ALU.add))
                    t["rw_grown"].wait(dve)
                for g, (g0, n) in enumerate(GROUPS):
                    nch, c0 = n // C, g0 // C
                    t["rw_mn"].next(dve)
                    m = ps[:, 2 + g, :].rearrange("p (x c v) -> p x c v", x=2, c=4)
                    for h in range(2):
                        r = slice(64 * h, 64 * h + 64)
                        tt(rmt[r, c0:c0 + nch, r], m[r, 0, 0:nch, :], K("ident64")[r].unsqueeze(1).to_broadcast([64, nch, 64]), ALU.add)
                        wl = rexp[r, 0, i, :].rearrange("p (c t) -> p c t", t=C)[:, c0:c0 + nch, C - 1:C].to_broadcast([64, nch, 64])
                        ins = tt(rnw[r, c0:c0 + nch, r], m[r, 1, 0:nch, :], wl)
                    t["rw_mns"].made(ins)
                t["rw_mns"].wait(dve)
                t["rw_state"].made(v.tensor_copy(rst[:, 1, :], rnw[:, 0, :]))
                for c in (8, 1, 2, 3, 4, 5, 6, 7):
                    t["rw_step"].next(dve)
                    t["rw_state"].made(stt(rst[:, c + 1 if c < 8 else 10, :], ps[:, 2 if c == 8 else 0, 0:P],
                                           rexp[:, 0, i, c * C + C - 1:c * C + C], rnw[:, c, :], ALU.mult, ALU.add))
                t["rw_z"].next(dve)
                t["rw_zs"].made(tt(rz[:, :], ps[:, 5, 0:T], rar[:, 1, :], ALU.add))
                link(tt(rt[:, 3, :], rsh[:, 0, :], rkn[:, :]))
                link(v.tensor_scalar(rt[:, 3, :], rt[:, 3, :], vec[:, bass.ds(i + VEC["rwkv_r_k"][0], 1)], None, ALU.mult))
                t["rw_ys"].next(dve)
                t["rw_yis"].next(dve)
                t["rw_y"].made(tt(rt[:, 0, :], ps[:, 4, 0:T], ryi[:, :], ALU.add))
                t["rw_mean"].next(dve)
                t["rw_centred"].made(stt(rt[:, 0, :], ps[:, 0, 0:T], -1.0 / 64, rt[:, 0, :], ALU.mult, ALU.add))
                link(tt(rt[:, 4, :], ps[:, 5, 0:T], rsh[:, 2, :]))
                t["rw_root"].next(dve)
                t["rw_centred"].wait(dve)
                link(v.reciprocal(rt[:, 3, :], rt[:, 2, :]))
                link(tt(rt[:, 0, :], rt[:, 0, :], rt[:, 3, :]))
                link(v.tensor_scalar(rt[:, 0, :], rt[:, 0, :], vec[:, bass.ds(i + VEC["rwkv_gn_g"][0], 1)],
                                     vec[:, bass.ds(i + VEC["rwkv_gn_b"][0], 1)], ALU.mult, ALU.add))
                link(tt(rt[:, 0, :], rt[:, 0, :], rt[:, 4, :], ALU.add))
                t["rw_out"].next(dve)
                t["rw_read"].made(tt(yT[:, bass.ds(i + 4, 1), :], rt[:, 0:1, :], gv[:, bass.ds(i, 1), :]))
            leave(4, RW_PER)
            t["mixed"].made(v.memset(epsb[:, 4:5], 0.0))
            for b in range(8):
                t["unit_used" if b % 2 else "first_block"].k += 1
                dve.wait_ge(sem["first_block"], 2 + b // 2)
                if b % 2:
                    dve.wait_ge(sem["unit_used"], 1 + 12 + 12 + b // 2 + 1)
                ins = tt(xT[:, b, :], ps[:, 1 + b % 4, 0:T], xT[:, b, :], ALU.add)
                t["abo_added"].made(ins)
            t["x_ready"].made(v.memset(epsb[:, 4:5], 0.0))
            norm(1)
            t["first_block"].k = 1 + 4
            t["unit_used"].k, t["unit_used"].base = 29, 0

            def ffn_up(pair):
                t["first_block"].k += 1
                t["unit_used"].k += 1
                for b in range(2):
                    t["ffn_silu"].next(dve)
                    t["unit_used" if b else "first_block"].next(dve)
                    t["ffn_made"].made(tt(gT[:, bass.ds(pair * 2 + b, 1), :], fsil[:, b:b + 1, :], ps[:, 2 + b:3 + b, 0:T]))

            ffn_up(0)
            ffn_up(1)
            with dve.Fori(0, 3) as i:
                enter(i, FFN_PER)
                for q in range(3):
                    ffn_up(i * 3 + (2 + q))
            leave(3, FFN_PER)
            for half in range(2):
                t["unit_used"].next(dve, 11)
                for n in range(4):
                    t["ffn_added"].made(tt(xT[:, 4 * half + n, :], ps[:, 4 - 4 * half + n, 0:T], xT[:, 4 * half + n, :], ALU.add))
            t["x_ready"].made(v.memset(epsb[:, 4:5], 0.0))
            norm(2)
            t["ret_done"].made(v.memset(epsb[:, 4:5], 0.0))
            with dve.Fori(0, 4) as i:
                enter(i, RET_PER)
                t["ret_evac"].next(dve, 8)
                cs, sn = (K(x).unsqueeze(1).to_broadcast([P, 2, T]) for x in ("cos", "sin"))
                qk = rqk[:, :, :].rearrange("p (a b) t -> p a b t", a=2)
                rot = rrot[:, :, :].rearrange("p (a b) t -> p a b t", a=2)
                tmp = rrt[:, :, :].rearrange("p (a b) t -> p a b t", a=2)
                tt(rot[:, :, 0], qk[:, :, 0], cs)
                tt(rot[:, :, 1], qk[:, :, 1], cs)
                tt(tmp[:, :, 0], qk[:, :, 1], sn)
                link(tt(tmp[:, :, 1], qk[:, :, 0], sn))
                tt(rot[:, :, 0], rot[:, :, 0], tmp[:, :, 0], ALU.subtract)
                link(tt(rot[:, :, 1], rot[:, :, 1], tmp[:, :, 1], ALU.add))
                c0 = const_layout()[0]["ret_q"][0]
                dec = const[:, bass.ds(i * 32 + c0, 32)].unsqueeze(1).to_broadcast([P, 2, TS])
                t["ret_rotated"].made(tt(rqs[:, :, :], rrot[:, 0:2, TP:T], dec))
                t["ret_evac"].k += 4
                t["ret_kturned"].next(dve)
                c0 = const_layout()[0]["ret_k"][0]
                for g, (g0, n) in enumerate(GROUPS):
                    ins = v.tensor_scalar(rK[0:n, g, :], ps[0:n, g // 2, 256 * (g % 2):256 * (g % 2) + 256],
                                          const[0:n, bass.ds(i + (c0 + 4 * g), 1)], None, ALU.mult)
                t["ret_ktok"].made(ins)
                t["ret_scores"].next(dve)
                c0 = const_layout()[0]["ret_mask"][0]
                m = [const[:, bass.ds(i * 256 + c0, n)] for n in (256, 128, TS)]
                tt(ratt[:, 0:256], ps[:, 2, 0:256], m[0])
                tt(ratt[:, 256:384], ps[:, 3, 0:128], m[1])
                t["ret_att"].made(tt(ratt[0:TS, 384:416], ps[0:TS, 3, 128:160], const[0:TS, bass.ds(i * 256 + c0, TS)]))
                t["ret_states"].next(dve)
                t["ret_buffer"].next(dve)
                c0 = const_layout()[0]["ret_q"][0]
                t["ret_stated_s"].made(stt(rS[:, 1, :, :], rS0[:, :, :], const[:, bass.ds(i * 32 + (c0 + 31), 1)], ps[:, 2:4, :], ALU.mult, ALU.add))
                t["ret_mean"].next(dve)
                t["ret_osb"].next(dve)
                t["ret_centred"].made(stt(ro[:, :, :], ps[:, 0, 0:T].unsqueeze(1).to_broadcast([P, 4, T]), -1.0 / 512, ro[:, :, :], ALU.mult, ALU.add))
                t["ret_root"].next(dve)
                link(v.reciprocal(rstd[:, 1, :], rstd[:, 0, :]))
                t["ret_centred"].wait(dve)
                link(tt(ro[:, :, :], ro[:, :, :], rstd[:, 1, :].unsqueeze(1).to_broadcast([P, 4, T])))
                for j in range(4):
                    ins = v.tensor_scalar(ro[:, j, :], ro[:, j, :], vec[:, bass.ds(i * 4 + (VEC["ret_gn_g"][0] + j), 1)],
                                          vec[:, bass.ds(i * 4 + (VEC["ret_gn_b"][0] + j), 1)], ALU.mult, ALU.add)
                link(ins)
                t["ret_evac"].wait(dve)
                t["ret_done"].made(tt(yR[:, bass.ds(i * 4, 4), :], ro[:, :, :], rgf[:, :, :]))
            leave(4, RET_PER)
            for b in range(8):
                if b % 2 == 0:
                    t["unit_used"].next(dve, 2)
                t["reto_added"].made(tt(xT[:, b, :], ps[:, 3 + b % 4, 0:T], xT[:, b, :], ALU.add))
            t["x_ready"].made(v.memset(epsb[:, 4:5], 0.0))
            dve.wait_ge(sem["ret_stored"], 32 * 4)
            norm(3)
            t["logits"].next(dve)
            for g, (g0, n) in enumerate(GROUPS):
                ins = v.tensor_reduce(small[0:n, g:g + 1], ps[0:n, 0, 8 * g:8 * g + 8], AX_X, ALU.max)
            link(ins)
            for g, (g0, n) in enumerate(GROUPS):
                ins = v.tensor_scalar(prob[0:n, g, :], ps[0:n, 0, 8 * g:8 * g + 8], small[0:n, g:g + 1], None, ALU.subtract)
            t["logits_centred"].made(ins)
            t["logits_exp"].next(dve)
            for g, (g0, n) in enumerate(GROUPS):
                ins = v.tensor_reduce(small[0:n, 3 + g:4 + g], prob[0:n, g, :], AX_X, ALU.add)
            link(ins)
            for g, (g0, n) in enumerate(GROUPS):
                ins = v.reciprocal(small[0:n, 6 + g:7 + g], small[0:n, 3 + g:4 + g])
            link(ins)
            for g, (g0, n) in enumerate(GROUPS):
                ins = v.tensor_scalar(prob[0:n, g, :], prob[0:n, g, :], small[0:n, 6 + g:7 + g], None, ALU.mult)
            link(ins)
            for g, (g0, n) in enumerate(GROUPS):
                ins = v.max(top[0:n, g, :], prob[0:n, g, :])
            link(ins)
            for g, (g0, n) in enumerate(GROUPS):
                ins = v.max_index(topi[0:n, g, :], top[0:n, g, :], prob[0:n, g, :])
            link(ins)
            for g, (g0, n) in enumerate(GROUPS):
                ins = v.tensor_copy(topf[0:n, g, 0:2], topi[0:n, g, 0:2])
            link(ins)
            for g, (g0, n) in enumerate(GROUPS):
                v.tensor_scalar(pick[0:n, g, 0:NEXP], K("cols", 0, 8)[0:n], topf[0:n, g, 0:1], None, ALU.is_equal)
                ins = v.tensor_scalar(gate[0:n, g, :], K("cols", 0, 8)[0:n], topf[0:n, g, 1:2], None, ALU.is_equal)
            link(ins)
            for g, (g0, n) in enumerate(GROUPS):
                ins = tt(pick[0:n, g, 0:NEXP], pick[0:n, g, 0:NEXP], gate[0:n, g, :], ALU.add)
                tt(small[0:n, 9 + g:10 + g], top[0:n, g, 0:1], top[0:n, g, 1:2], ALU.add)
            t["picked"].made(v.memset(epsb[:, 4:5], 0.0))
            t["picked"].wait(dve)
            for g, (g0, n) in enumerate(GROUPS):
                ins = v.reciprocal(small[0:n, 12 + g:13 + g], small[0:n, 9 + g:10 + g])
            link(ins)
            for g, (g0, n) in enumerate(GROUPS):
                ins = stt(gate[0:n, g, :], prob[0:n, g, :], small[0:n, 12 + g:13 + g], pick[0:n, g, 0:NEXP], ALU.mult, ALU.mult)
            link(ins)
            t["placed"].next(dve)
            for g, (g0, n) in enumerate(GROUPS):
                v.tensor_copy(place[0:n, g, 0:NEXP], ps[0:n, 7, 8 * g:8 * g + 8])
                v.tensor_scalar(place[0:n, g, NEXP:NEXP + 1], ps[0:n, 7, 8 * g:8 * g + 1], float(CAP), None, ALU.subtract)
                v.tensor_copy(pick[0:n, g, NEXP:NEXP + 1], pick[0:n, g, 0:1])
            link(v.tensor_reduce(small[:, 0:1], ps[:, 7, 32:40], AX_X, ALU.max))
            link(v.tensor_scalar(small[:, 1:2], small[:, 0:1], float(CAP), 1.0, ALU.is_gt, ALU.add))
            link(stt(small[:, 2:3], small[:, 0:1], 2.0 * CAP, small[:, 1:2], ALU.is_gt, ALU.add))
            t["rounds_known"].made(v.tensor_copy(rounds[0:1, 0:1], small[0:1, 2:3]))
            t["rounds_known"].wait(dve)
            t["slot_free"].k = RINGX
            def take(e):
                for g, (g0, n) in enumerate(GROUPS):
                    ins = v.tensor_scalar(take_f[0:n, g, :], K("cols", 0, CAP)[0:n], place[0:n, g, bass.ds(e, 1)], pick[0:n, g, bass.ds(e, 1)], ALU.is_equal, ALU.mult)
                return ins

            def add(k):
                t["x_out"].next(dve)
                t["x_added"].made(tt(xT[:, k, :], ps[:, 4 + k % 2, 0:T], xT[:, k, :], ALU.add))

            t["x_give"].made(take(0))
            t["x_taken"].k += 1
            v.memset(yx[:, :], 0.0)
            t["x_y"].made(v.memset(giveT[:, :], 0.0))
            n_rounds = count_rounds(dve)
            with dve.Fori(0, n_rounds) as r:
                with dve.Fori(0, NEXP) as e:
                    enter(r * NEXP + e, X_PER)
                    t["x_taken"].wait(dve)
                    for g, (g0, n) in enumerate(GROUPS):
                        v.tensor_scalar(give_f[0:n, g, :], K("cols", 0, CAP)[0:n], place[0:n, g, bass.ds(e, 1)], gate[0:n, g, bass.ds(e, 1)], ALU.is_equal, ALU.mult)
                    t["x_give"].made(take(e + 1))
                    for j in range(KF // 2):
                        t["x_silu"].next(dve)
                        t["slot_free"].next(dve, 2)
                        t["x_read"].made(tt(gx_[:, 2 * j:2 * j + 2, :], xsil[:, j % 2, :].rearrange("p (c n) -> p c n", c=2),
                                            ps[:, 2 * (j % 2) + 1, 0:2 * CAP].rearrange("p (c n) -> p c n", c=2)))
                        if 1 <= j <= 4:
                            add(2 * j - 2)
                            add(2 * j - 1)
                    t["slot_free"].k += 11
                for g, (g0, n) in enumerate(GROUPS):
                    ins = v.tensor_scalar(place[0:n, g, :], place[0:n, g, :], float(CAP), None, ALU.subtract)
                ins.then_inc(sem["places_moved"], 1)
                dve.wait_ge(sem["places_moved"], r + 1)
            for name in X_PER:
                t[name].k = 0
            enter(n_rounds * NEXP, X_PER)
            for k in range(KD):
                add(k)
            t["x_ready"].made(v.memset(epsb[:, 4:5], 0.0))
            norm(4)

        @block.gpsimd
        def _(pool):
            pool.wait_ge(sem["gla_read"], 2)
            pool.wait_ge(sem["gla_states"], 2)
            pool.wait_ge(sem["rw_out"], 4)
            pool.wait_ge(sem["shifts_out"], 1)
            for s2, (og, orw, osh) in enumerate(((o[2], o[3], o[4]), (o[6], o[7], o[8]))):
                pool.dma_start(og[0, 0].rearrange("(q h) k v -> (h k) q v", q=2), gla_out[:, :, s2, :]).then_inc(sem["stored"], 16)
                pool.dma_start(orw[0, 0].rearrange("(q h) v k -> (h v) q k", q=4), rw_out[:, :, s2, :]).then_inc(sem["stored"], 16)
                pool.dma_start(osh[0, 0].rearrange("a (j p) -> (a j) p", p=P), shifto[14 * s2:14 * s2 + 14, :]).then_inc(sem["stored"], 16)
            pool.wait_ge(sem["normed"], 3)
            pool.dma_start(rS0[:, :, :], a["state_ret"][0, 0, 0].rearrange("(x k) v -> k x v", x=2)).then_inc(sem["ret_state_in"], 16)
            pool.sem_inc(sem["ret_buffer"], 1)

            def store(i):
                for s2, dst in enumerate((o[5], o[9])):
                    pool.dma_start(dst[0, 0, bass.ds(i, 1)][0].rearrange("(x k) v -> k x v", x=2), rS[:, s2, :, :]).then_inc(sem["ret_stored"], 16)

            with pool.Fori(0, 3) as i:
                pool.wait_ge(sem["ret_stated_p"], i + 1)
                pool.wait_ge(sem["ret_stated_s"], i + 1)
                store(i)
                pool.wait_ge(sem["ret_o"], i + 1)
                pool.dma_start(rS0[:, :, :], a["state_ret"][0, 0, bass.ds(i + 1, 1)][0].rearrange("(x k) v -> k x v", x=2)).then_inc(sem["ret_state_in"], 16)
                pool.wait_ge(sem["ret_stored"], i * 32 + 32)
                pool.sem_inc(sem["ret_buffer"], 1)
            pool.wait_ge(sem["ret_stated_p"], 4)
            pool.wait_ge(sem["ret_stated_s"], 4)
            store(3)
            pool.wait_ge(sem["stored"], 16 * 6)
            pool.wait_ge(sem["ret_stored"], 32 * 4)


_OUTS = [(1, TP, D), (1, TS, D), (1, 1, 4, 64, 128), (1, 1, 8, 64, 64), (1, 1, 1, 1792), (1, 1, 4, 256, 512),
         (1, 1, 4, 64, 128), (1, 1, 8, 64, 64), (1, 1, 1, 1792), (1, 1, 4, 256, 512)]


def kernel(**inputs):
    import concourse.bacc as bacc
    from concourse.bass_utils import run_bass_kernel_spmd

    nc = bacc.Bacc("TRN2", target_bir_lowering=False, num_devices=1)
    arrays, args = {}, {}
    for name, value in inputs.items():
        arr = np.ascontiguousarray(value)
        arrays[f"in_{name}"] = arr
        args[name] = nc.dram_tensor(f"in_{name}", arr.shape, F32, kind="ExternalInput").ap()
    arrays["in_const"] = const_array()
    args["const"] = nc.dram_tensor("in_const", arrays["in_const"].shape, F32, kind="ExternalInput").ap()
    outs = [nc.dram_tensor(f"out_{i}", shape, F32, kind="ExternalOutput").ap() for i, shape in enumerate(_OUTS)]
    program(nc, args, outs)
    r = run_bass_kernel_spmd(nc, [arrays], core_ids=[0])
    return tuple(r.results[0][f"out_{i}"] for i in range(len(_OUTS)))
```

```python
from contextlib import ExitStack

import numpy as np
import concourse.bass as bass
from concourse import mybir
from concourse.alu_op_type import AluOpType as ALU

ACT = mybir.ActivationFunctionType
F32 = mybir.dt.float32
I32 = mybir.dt.int32
AX_X = mybir.AxisListType.X

P = 128
D, KD = 1024, 8
TP, TS = 256, 32
T = TP + TS
C = 32
NCH = T // C
GROUPS = [(0, 128), (128, 128), (256, 32)]
DFF = 2816
KF = DFF // P
NEXP = 8
QA, KA, VA, GA, OGA = 0, 256, 512, 1024, 1040
B0 = 1552
RB, KB, VB, LORA = B0, B0 + 512, B0 + 1024, B0 + 1536
RING = 3
RINGX = 11
CAP = 112
EPS = 1e-6
SMALL_LOADS = 8


def const_layout():
    at, n = {}, 0
    for name, w in (("ident", 128), ("ones", 128), ("heads", 128), ("incl_t", 256), ("strict_incl_t", 256),
                    ("strict", 128), ("scan", T), ("chunk", 4), ("ident64", 64), ("cos", T), ("sin", T),
                    ("ret_mask", 4 * 256), ("ret_k", 3 * 4), ("ret_q", 4 * 32), ("cols", 128), ("before", 128)):
        at[name] = (n, w)
        n += w
    return at, n


def const_array():
    at, n = const_layout()
    c = np.zeros((P, n), np.float32)

    def put(name, a):
        o, w = at[name]
        c[:, o:o + w] = np.asarray(a, np.float64).reshape(P, w).astype(np.float32)

    i = np.arange(P)
    same = (i[:, None] // C) == (i[None, :] // C)
    put("ident", np.eye(P))
    put("ones", np.ones((P, P)))
    put("heads", (i[:, None] // 64) == (i[None, :] // 64))
    incl_t = same & (i[:, None] <= i[None, :])
    strict_t = same & (i[:, None] < i[None, :])
    put("incl_t", np.concatenate([incl_t, incl_t], 1))
    put("strict_incl_t", np.concatenate([strict_t, incl_t], 1))
    put("strict", same & (i[:, None] > i[None, :]))
    put("scan", np.tile((np.arange(T) % C != 0)[None], (P, 1)))
    put("chunk", (i[:, None] // C) == np.arange(4)[None])
    put("ident64", (i[:, None] % 64) == np.arange(64)[None])
    inv = (1.0 / (np.float32(10000.0) ** (np.arange(0, 256, 2, dtype=np.float32) / np.float32(256)))).astype(np.float32)
    ang = (inv[:, None] * np.arange(T, dtype=np.float32)[None]).astype(np.float32).astype(np.float64)
    put("cos", np.cos(ang))
    put("sin", np.sin(ang))
    gam = 1.0 - 2.0 ** (-5.0 - np.arange(4))
    d = np.arange(256)[None, :] - i[:, None]
    put("ret_mask", np.stack([np.where(d >= 0, g ** np.maximum(d, 0), 0) / 16 for g in gam], 1))
    last = np.array([255, 127, 31])
    k = np.zeros((P, 3, 4))
    for g in range(3):
        k[:, g, :] = gam[None] ** np.maximum(last[g] - i, 0)[:, None] / 16
    put("ret_k", k)
    put("ret_q", np.tile((gam[:, None] ** (np.arange(32)[None] + 1)).reshape(1, -1), (P, 1)))
    put("cols", np.tile(np.arange(P)[None], (P, 1)))
    put("before", i[:, None] < i[None, :])
    return c


ROWS = [("norm_mix", 16), ("norm_ffn", 16), ("norm_final", 8), ("gla_b_gate", 2), ("gla_norm", 1), ("rwkv_mu", 14),
        ("rwkv_w0", 4), ("rwkv_a0", 4), ("rwkv_k_k", 4), ("rwkv_k_a", 4), ("rwkv_r_k", 4), ("rwkv_gn_g", 4),
        ("rwkv_gn_b", 4), ("state_shift", 14), ("ret_gn_g", 16), ("ret_gn_b", 16)]
VEC = {}
_n = 0
for _name, _w in ROWS:
    if _name == "ret_gn_g":
        _n = P
    VEC[_name] = (_n, _w)
    _n += _w
NVEC = _n


class Tally:

    def __init__(self, sem, name=""):
        self.sem, self.name, self.base, self.k, self.i, self.per = sem, name, 0, 0, None, 0

    def enter(self, i, per):
        self.base, self.k, self.i, self.per = self.base + self.k, 0, i, per

    def leave(self, n):
        assert self.k in (0, self.per), (self.name, self.k, self.per)
        self.base, self.k, self.i = self.base + self.per * n, 0, None

    def value(self, d=0):
        v = self.base + self.k + d
        return v if self.i is None else self.i * self.per + v

    def low(self, d=0):
        return self.base + self.k + d

    def made(self, ins, n=1):
        ins.then_inc(self.sem, n)
        self.k += n
        return ins

    def wait(self, eng, d=0):
        eng.wait_ge(self.sem, self.value(d))

    def next(self, eng, n=1):
        self.k += n
        eng.wait_ge(self.sem, self.value())

    def link(self, eng, ins):
        self.made(ins)
        eng.wait_ge(self.sem, self.value())

SEMAPHORES = """
    unit_used in_ones in_x slot_free ret_stored rounds_known normed squares square_sums x_copied x_turned
    in_rows vec_turned first_block in_lora ga_block gate_in gate_blocks lora_in gate_out lora_out lora_mixed
    gla_evac gla_feats gla_scores gla_turned gla_vt gla_kx gla_updates gla_masked gla_states gla_o gla_osq
    gla_osum gla_read rw_ksq rw_ksum rw_ysq rw_var rw_out rw_state_in rw_state_turned rw_feats rw_turned
    rw_plain rw_state_put rw_tok rw_bkx rw_scores rw_scored rw_q rw_squared rw_power rw_grown rw_grow rw_evac
    rw_akv rw_x rw_gh rw_ghs rw_bonus rw_mn rw_z rw_yi rw_mns rw_state rw_step rw_zs rw_ys rw_final rw_y
    rw_mean rw_root shifts_turned mixed abo_added ffn_silu ffn_made ffn_added ret_osb ret_mean ret_osq ret_var
    ret_evac ret_root ret_vturned ret_rotated ret_kturned ret_scores ret_vtok ret_ktok ret_states ret_att
    ret_state_in ret_o ret_stated_p ret_stated_s reto_added ret_done logits frames_turned picked placed
    frames_tok x_taken x_added x_out x_give x_h x_read x_y x_ready y_turned roots in_const eps_set lora_raw
    lora_shifted act_chain gate_log gate_sums gate_exps decay_sums decay_exps gla_og gla_root rw_kroot rw_yis
    rw_centred shifts_out ret_centred ret_buffer logits_centred logits_exp x_silu y_copied y_stored dve_chain
    places_moved stored
"""

GLA_PER = dict(unit_used=6, gla_evac=6, gla_feats=1, gla_scores=1, gla_turned=3, gla_vt=3, gla_kx=3, gla_updates=3,
               gla_masked=1, gla_states=1, gla_o=1, gla_osq=1, gla_osum=1, gla_read=1, gla_og=1, gla_root=1, dve_chain=12)
RW_PER = dict(unit_used=3, rw_evac=3, rw_ksq=1, rw_ksum=1, rw_state_in=1, rw_state_turned=1, rw_feats=1, rw_turned=3,
              rw_plain=1, rw_state_put=1, rw_tok=3, rw_bkx=3, rw_scores=3, rw_scored=3, rw_q=1, rw_squared=12, rw_power=12,
              rw_grow=12, rw_grown=12, rw_akv=1, rw_x=1, rw_gh=1, rw_ghs=1, rw_mn=3, rw_z=1, rw_yi=1, rw_mns=3, rw_step=8,
              rw_state=9, rw_zs=1, rw_ys=1, rw_final=1, rw_y=1, rw_mean=1, rw_ysq=1, rw_var=1, rw_bonus=1, rw_kroot=1,
              rw_yis=1, rw_out=1, rw_centred=1, rw_root=1, dve_chain=17)
FFN_PER = dict(unit_used=6, first_block=6, ffn_made=6, ffn_silu=6)
DOWN_PER = dict(unit_used=3)
RET_PER = dict(unit_used=6, first_block=6, ret_done=1, ret_evac=12, ret_vturned=1, ret_rotated=1, ret_kturned=1, ret_scores=1,
               ret_vtok=1, ret_ktok=1, ret_att=1, ret_state_in=16, ret_o=1, ret_states=1, ret_stated_p=1, ret_stated_s=1, ret_osb=1, ret_mean=1,
               ret_osq=1, ret_var=1, ret_centred=1, ret_root=1, ret_buffer=1, dve_chain=5)
X_PER = dict(x_give=1, x_taken=1, x_h=1, x_read=11, slot_free=33, x_y=1, x_added=8, x_out=8, x_silu=11)


def program(nc, a, o):
    with ExitStack() as ctx:
        layer0 = ExitStack()

        def sb(name, shape, where=ctx, dt=F32):
            return where.enter_context(nc.sbuf_tensor(name, shape, dt))

        ps = ctx.enter_context(nc.psum_tensor("ps", [P, 8, 512], F32))

        sem = {}
        for name in SEMAPHORES.split():
            sem[name] = ctx.enter_context(nc.semaphore(name))
        x_arrived = [ctx.enter_context(nc.semaphore(f"expert_weights_arrived_{s}")) for s in range(RINGX)]
        arrived = [ctx.enter_context(nc.semaphore(f"weights_arrived_{s}")) for s in range(RING)]

        ring = sb("ring", [P, RING, KD * 256])
        const = sb("const", [P, const_layout()[1]])
        rows = sb("rows", [P, 2, P])
        vec = sb("vec", [P, NVEC])
        omka = sb("omka", [P, 4])
        xT = sb("xT", [P, KD, T])
        hT = sb("hT", [P, KD, T])
        yT = sb("yT", [P, KD, T])
        rstd = sb("rstd", [P, 2, T])
        w_router = sb("w_router", [P, KD, NEXP])

        def K(name, lo=0, n=None):
            at, w = const_layout()[0][name]
            return const[:, at + lo:at + (w if n is None else lo + n)]

        def V(name, j=0, n=1):
            return vec[:, VEC[name][0] + j:VEC[name][0] + j + n]

        epsb = sb("epsb", [P, 8])

        def eps(e):
            return epsb[:, (EPS, 64e-5, None, 1e-5).index(e):][:, 0:1]

        def one():
            return epsb[:, 2:3]

        def chunks(ap):
            return ap.rearrange("p (c t) -> p c t", t=C)

        shifto = sb("shifto", [28, P])
        gla_out = sb("gla_out", [P, 2, 2, P])
        rw_out = sb("rw_out", [P, 4, 2, 64])
        L = layer0
        w_ga = sb("w_ga", [P, KD, 16], L)
        w_gate = sb("w_gate", [16, 256], L)
        w_wa = sb("w_wa", [P, 512], L)
        w_g = sb("w_g", [P, 512], L)
        lora = sb("lora", [P, 6, T], L)
        gaT = sb("gaT", [16, T], L)
        gend = sb("gend", [P, 2, NCH], L)
        lw = sb("lw", [P, 4, T], L)
        rexp = sb("rexp", [P, 3, 4, T], L)
        av = sb("av", [P, 4, T], L)
        gv = sb("gv", [P, 4, T], L)
        shiftb = sb("shiftb", [P, 2, 14], L)
        gla_in = sb("gla_in", [P, 2, P], L)
        rw_in = sb("rw_in", [P, 4, 64], L)
        G = ExitStack()
        xrow = sb("xrow", [P, 3, D], G)
        gz = sb("gz", [P, 3, 2, T], G)
        gexp = sb("gexp", [P, 4, 2, T], G)
        gx = sb("gx", [P, 6, T], G)
        gf = sb("gf", [P, 4, T], G)
        gatt = sb("gatt", [P, 2, T], G)
        gvt = sb("gvt", [P, 3, 2, P], G)
        gkx = sb("gkx", [P, 3, 4, P], G)
        gst = sb("gst", [P, 11, P], G)
        go = sb("go", [P, 4, T], G)
        G.close()
        rx = sb("rx", [P, 3, T], L)
        rp = sb("rp", [P, 3, T], L)
        rsh = sb("rsh", [P, 3, T], L)
        rt = sb("rt", [P, 5, T], L)
        rkn = sb("rkn", [P, T], L)
        rbonus = sb("rbonus", [P, T], L)
        rkeep = sb("rkeep", [P, 2, T], L)
        rar = sb("rar", [P, 2, T], L)
        rbk = sb("rbk", [P, 2, T], L)
        rsc = sb("rsc", [P, 3, 2, 2, 256], L)
        rpw = sb("rpw", [P, 2, 3, 2, 2, P], L)
        rq = sb("rq", [P, 2, 3, 2, P], L)
        rvt = sb("rvt", [P, 3, P], L)
        rax = sb("rax", [P, 3, 2, 2, 64], L)
        rbx = sb("rbx", [P, 3, 4, P], L)
        rkx = sb("rkx", [P, 3, 4, P], L)
        rgh = sb("rgh", [P, 3, 2, P], L)
        rmt = sb("rmt", [P, NCH, P], L)
        rnw = sb("rnw", [P, NCH, P], L)
        rz = sb("rz", [P, T], L)
        ryi = sb("ryi", [P, T], L)
        rst = sb("rst", [P, 11, P], L)
        rsi = sb("rsi", [P, P], L)
        L.close()
        F = ExitStack()
        gT = sb("gT", [P, KF, T], F)
        fsil = sb("fsil", [P, 2, T], F)
        F.close()
        R = ExitStack()
        yR = sb("yR", [P, 16, T], R)
        rqk = sb("rqk", [P, 4, T], R)
        rvf = sb("rvf", [P, 4, T], R)
        rgf = sb("rgf", [P, 4, T], R)
        rrot = sb("rrot", [P, 4, T], R)
        rrt = sb("rrt", [P, 4, T], R)
        rqs = sb("rqs", [P, 2, TS], R)
        rV = sb("rV", [P, 3, 512], R)
        rK = sb("rK", [P, 3, 256], R)
        ratt = sb("ratt", [P, 416], R)
        ro = sb("ro", [P, 4, T], R)
        rosq = sb("rosq", [P, 4, T], R)
        rS0 = sb("rS0", [P, 2, 512], R)
        rS = sb("rS", [P, 2, 2, 512], R)
        R.close()
        X = ExitStack()
        xring = sb("xring", [P, RINGX, KD * 256], X)
        htok = sb("htok", [P, 3, D], X)
        top = sb("top", [P, 3, 8], X)
        topi = sb("topi", [P, 3, 8], X, mybir.dt.uint32)
        topf = sb("topf", [P, 3, 8], X)
        prob = sb("prob", [P, 3, NEXP], X)
        pick = sb("pick", [P, 3, NEXP + 1], X)
        gate = sb("gate", [P, 3, NEXP], X)
        place = sb("place", [P, 3, NEXP + 1], X)
        small = sb("small", [P, 16], X)
        counts = sb("counts", [P, NEXP], X)
        rounds = sb("rounds", [1, 1], X, I32)
        take_f = sb("take_f", [P, 3, CAP], X)
        give_f = sb("give_f", [P, 3, CAP], X)
        giveT = sb("giveT", [CAP, T], X)
        hx = sb("hx", [P, KD, CAP], X)
        gx_ = sb("gx_", [P, KF, CAP], X)
        xsil = sb("xsil", [P, 2, 2 * CAP], X)
        yx = sb("yx", [CAP, D], X)
        X.close()
        ytok = htok

        W_IN = a["ab_w_in"][0].rearrange("(k p) n -> p k n", p=P)
        W_OUT = a["ab_w_out"][0].rearrange("(k p) n -> p k n", p=P)
        W1, W3, W2, W_RET, W_RETO = (a[n][0].rearrange("(k p) n -> p k n", p=P) for n in ("ffn_w1", "ffn_w3", "ffn_w2", "ret_w_in", "ret_w_out"))
        X1, X3, X2 = (a[n][0].rearrange("e (k p) n -> e p k n", p=P) for n in ("moe_w1", "moe_w3", "moe_w2"))

        def norm_columns(r):
            return [V("norm_mix", 0, 8), V("norm_ffn", 0, 8), V("norm_mix", 8, 8), V("norm_ffn", 8, 8), V("norm_final", 0, 8)][r]

        def count_rounds(eng):
            return eng.value_load(rounds[0:1, 0:1], min_val=1, max_val=-(-T // CAP))

        block = ctx.enter_context(nc.Block())

        @block.sync
        def _(sp):
            used = Tally(sem["unit_used"], "unit_used")
            unit = [0, None, 0]

            def load(parts):
                sent, i, per = unit
                if sent >= RING or i is not None:
                    need = max(sent - RING + 1, 1)
                    sp.wait_ge(sem["unit_used"], need if i is None else i * per + need)
                slot = sent % RING
                for n, (dst, src) in enumerate(parts):
                    sp.dma_start(dst(slot), src).then_inc(arrived[slot], 16)
                unit[0] += 1

            def columns(w, c0, n, k0=0):
                return [(lambda s: ring[:, s, 0:KD * n].rearrange("p (k n) -> p k n", k=KD), w[:, k0:k0 + KD, bass.ds(c0, n)])]

            sp.dma_start(const[:, 0:256], a["const"][:, 0:256]).then_inc(sem["in_ones"], 16)
            for g in range(2):
                sp.dma_start(xrow[:, g, :], a["x_prompt"][0, g * P:(g + 1) * P, :]).then_inc(sem["in_x"], 16)
            sp.dma_start(xrow[0:TS, 2, :], a["x_sample"][0]).then_inc(sem["in_x"], 16)
            load(columns(W_IN, LORA, 256))
            with sp.Fori(0, 2) as i:
                unit[1:] = [i, 6]
                for c in (QA, KA):
                    load(columns(W_IN, i * 128 + c, 128))
                for c in (VA, VA + 128, OGA, OGA + 128):
                    load(columns(W_IN, i * 256 + c, 128))
            unit[:] = [unit[0] + 6, None, 0]
            for c in (RB, KB, VB):
                load(columns(W_IN, c, 128))
            with sp.Fori(0, 3) as i:
                unit[1:] = [i, 3]
                for c in (RB, KB, VB):
                    load(columns(W_IN, i * 128 + (c + 128), 128))
            unit[:] = [unit[0] + 6, None, 0]
            for j in range(4):
                load(columns(W_OUT, 256 * j, 256))

            for j in range(2):
                load(columns(W1, 256 * j, 256))
                load(columns(W3, 256 * j, 256))
            with sp.Fori(0, 3) as i:
                unit[1:] = [i, 18 // 3]
                for q in range(3):
                    load(columns(W1, i * 768 + (512 + 256 * q), 256))
                    load(columns(W3, i * 768 + (512 + 256 * q), 256))
            unit[:] = [unit[0] + 12, None, 0]

            def down(k, half):
                return [(lambda s: ring[:, s, 0:1024].rearrange("p (k n) -> p k n", k=2), W2[:, k, 512 * half:512 * half + 512])]

            for half in range(2):
                load(down(slice(0, 2), half))
                with sp.Fori(0, 3) as i:
                    unit[1:] = [i, 3]
                    for q in range(3):
                        load(down(bass.ds(i * 6 + (2 + 2 * q), 2), half))
                unit[:] = [unit[0] + 6, None, 0]
                load(down(slice(20, 22), half))
            def head(h):
                for c in (0, 1024):
                    load(columns(W_RET, h(256) + c, 256))
                for c in (2048, 2304, 4096, 4352):
                    load(columns(W_RET, h(512) + c, 256))

            head(lambda w: 0)
            with sp.Fori(0, 3) as i:
                unit[1:] = [i, 6]
                head(lambda w: i * w + w)
            unit[:] = [unit[0] + 12, None, 0]
            for half in range(2):
                for kh in range(2):
                    for j in (2 * half, 2 * half + 1):
                        load(columns(W_RETO, 256 * j, 256, KD * kh))
            sp.wait_ge(sem["slot_free"], RINGX)
            sp.wait_ge(sem["ret_stored"], 32 * 4)
            sp.wait_ge(sem["rounds_known"], 1)
            with sp.Fori(0, count_rounds(sp)) as r:
                with sp.Fori(0, NEXP) as e:
                    turn = r * NEXP + e
                    for k in range(33):
                        sp.wait_ge(sem["slot_free"], turn * 33 + (k + 1))
                        if k < 22:
                            w = X3 if k % 2 else X1
                            dst = xring[:, k % RINGX, :].rearrange("p (k n) -> p k n", k=KD)
                            src = w[bass.ds(e, 1), :, :, 256 * (k // 2):256 * (k // 2) + 256][0]
                        else:
                            dst = xring[:, k % RINGX, :].rearrange("p (k n) -> p k n", k=2)
                            src = X2[bass.ds(e, 1), :, 2 * (k - 22):2 * (k - 22) + 2, :][0]
                        sp.dma_start(dst, src).then_inc(x_arrived[k % RINGX], 16)

        @block.tensor
        def _(pe):
            t = {n: Tally(s, n) for n, s in sem.items()}
            unit = [0, None, 0]

            def take():
                k, i, per = unit
                v = 16 * (k // RING + 1)
                pe.wait_ge(arrived[k % RING], v if i is None else i * (16 * per // RING) + v)
                unit[0] += 1
                return k % RING

            def gemm(out, slot, c0, width, rhs, start=True, stop=True, ks=KD, m=P, fresh=False):
                w = ring[:, slot, 0:ks * width].rearrange("p (k n) -> p k n", k=ks)
                for k in range(ks):
                    if fresh:
                        t["normed"].next(pe)
                    ins = nc.tensor.matmul(out, w[:, k, c0:c0 + m], rhs[:, k, :], start=start and k == 0, stop=stop and k == ks - 1)
                return ins

            def enter(i, per, units):
                for n, p in per.items():
                    t[n].enter(i, p)
                unit[1:] = [i, units]

            def leave(n, per):
                for name in per:
                    t[name].leave(n)
                unit[0] += (n - 1) * unit[2]
                unit[1:] = [None, 0]

            def norm():
                for k in range(KD):
                    if k % 4 == 0:
                        t["squares"].next(pe)
                    ins = nc.tensor.matmul(ps[:, 7, 0:T], K("ones"), yT[:, k, :], start=k == 0, stop=k == KD - 1)
                t["square_sums"].made(ins)

            pe.wait_ge(sem["in_ones"], 16)
            pe.wait_ge(sem["in_x"], 48)
            for k in range(KD):
                if k >= 4:
                    pe.wait_ge(sem["x_copied"], k - 3)
                for g, (g0, n) in enumerate(GROUPS):
                    ins = nc.tensor.transpose(ps[:, 2 + k % 4, g0:g0 + n], xrow[0:n, g, k * P:(k + 1) * P], K("ident")[0:n, 0:n])
                t["x_turned"].made(ins)
            pe.wait_ge(sem["in_rows"], 16 * len(ROWS))
            nc.tensor.transpose(ps[:, 0, 0:99], rows[0:99, 0, :], K("ident")[0:99, 0:99])
            t["vec_turned"].made(nc.tensor.transpose(ps[:, 1, 0:32], rows[0:32, 1, :], K("ident")[0:32, 0:32]))
            norm()

            s = take()
            t["first_block"].made(gemm(ps[:, 0, 0:T], s, 0, 256, hT, fresh=True))
            t["unit_used"].made(gemm(ps[:, 1, 0:T], s, 128, 256, hT))
            pe.wait_ge(sem["in_lora"], 16 * SMALL_LOADS)
            for k in range(KD):
                ins = nc.tensor.matmul(ps[0:16, 2, 0:T], w_ga[:, k, :], hT[:, k, :], start=k == 0, stop=k == KD - 1)
            t["ga_block"].made(ins)
            t["gate_in"].next(pe)
            for j in range(2):
                ins = nc.tensor.matmul(ps[:, 3 + j, 0:T], w_gate[:, j * P:(j + 1) * P], gaT[:, :], start=True, stop=True)
            t["gate_blocks"].made(ins)
            t["lora_in"].next(pe)
            for j in range(4):
                b = 3 * (j % 2)
                if j == 1:
                    pe.wait_ge(sem["gate_out"], 1)
                if j >= 2:
                    pe.wait_ge(sem["lora_out"], j - 1)
                nc.tensor.matmul(ps[:, b, 0:T], w_wa[0:64, j * P:(j + 1) * P], lora[0:64, 4, :], start=True, stop=True)
                nc.tensor.matmul(ps[:, b + 1, 0:T], w_wa[64:128, j * P:(j + 1) * P], lora[64:128, 4, :], start=True, stop=True)
                t["lora_mixed"].made(nc.tensor.matmul(ps[:, b + 2, 0:T], w_g[:, j * P:(j + 1) * P], lora[:, 5, :], start=True, stop=True))
            t["lora_out"].k = 4
            t["lora_out"].wait(pe)

            with pe.Fori(0, 2) as i:
                enter(i, GLA_PER, 6)
                for b in range(6):
                    if b >= 2:
                        t["gla_evac"].wait(pe, b - 1)
                    s = take()
                    t["unit_used"].made(gemm(ps[:, b % 2, 0:T], s, 0, 128, hT))
                t["gla_evac"].k += 6
                t["gla_feats"].next(pe)
                for h in range(2):
                    for g, (g0, n) in enumerate(GROUPS):
                        r = slice(64 * h, 64 * h + 64)
                        ins = nc.tensor.matmul(ps[0:n, 2 + h, g0:g0 + n], gf[r, 1, g0:g0 + n], gf[r, 0, g0:g0 + n], start=True, stop=True)
                t["gla_scores"].made(ins)
                t["gla_evac"].wait(pe)
                for g, (g0, n) in enumerate(GROUPS):
                    for j, src in enumerate((gf[:, 3, g0:g0 + n], gx[:, 2, g0:g0 + n], gx[:, 3, g0:g0 + n])):
                        ins = nc.tensor.transpose(ps[0:n, 4 + g, j * P:(j + 1) * P], src, K("ident"))
                    t["gla_turned"].made(ins)
                for g, (g0, n) in enumerate(GROUPS):
                    t["gla_vt"].next(pe)
                    t["gla_kx"].next(pe)
                    b = (7, 4, 5)[g]
                    for h in range(2):
                        for c in range(n // C):
                            ins = nc.tensor.matmul(ps[64 * h:64 * h + 64, b, c * P:(c + 1) * P],
                                                   gkx[0:n, g, c, 64 * h:64 * h + 64], gvt[0:n, g, h, :], start=True, stop=True)
                    t["gla_updates"].made(ins)
                t["gla_masked"].next(pe)
                t["gla_states"].next(pe)
                for h, b in ((0, 6), (1, 2)):
                    r = slice(64 * h, 64 * h + 64)
                    for g, (g0, n) in enumerate(GROUPS):
                        nc.tensor.matmul(ps[:, b, g0:g0 + n], gvt[0:n, g, h, :], gatt[0:n, h, g0:g0 + n], start=True, stop=False, skip_group_check=True)
                        for c in range(n // C):
                            cc = g0 // C + c
                            slot = cc if cc < 8 else 9
                            ins = nc.tensor.matmul(ps[:, b, cc * C:(cc + 1) * C], gst[r, slot, :], gf[r, 2, cc * C:(cc + 1) * C],
                                                   start=False, stop=c == n // C - 1, skip_group_check=True)
                t["gla_o"].made(ins)
                t["gla_osq"].next(pe)
                nc.tensor.matmul(ps[:, 3, 0:T], K("ones"), go[:, 0, :], start=True, stop=True)
                t["gla_osum"].made(nc.tensor.matmul(ps[:, 4, 0:T], K("ones"), go[:, 1, :], start=True, stop=True))
                t["gla_read"].next(pe)
            leave(2, GLA_PER)

            def rw_block(b):
                s = take()
                t["unit_used"].made(gemm(ps[:, b % 2, 0:T], s, 0, 128, hT))

            def rw_keys():
                t["rw_ksq"].next(pe)
                t["rw_ksum"].made(nc.tensor.matmul(ps[:, 7, 0:T], K("heads"), rt[:, 1, :], start=True, stop=True))

            def rw_var():
                t["rw_ysq"].next(pe)
                t["rw_var"].made(nc.tensor.matmul(ps[:, 4, 0:T], K("heads"), rt[:, 1, :], start=True, stop=True))

            def rw_front(first):
                if not first:
                    t["rw_out"].next(pe)
                t["rw_state_in"].next(pe)
                t["rw_state_turned"].made(nc.tensor.transpose(ps[:, 3, 0:P], rsi[:, :], K("ident")))
                t["rw_feats"].next(pe)
                for g, (g0, n) in enumerate(GROUPS):
                    for j, src in enumerate((rar[:, 0], rbk[:, 0], rbk[:, 1], rsh[:, 2])):
                        ins = nc.tensor.transpose(ps[0:n, 5 + g, j * P:(j + 1) * P], src[:, g0:g0 + n], K("ident"))
                    t["rw_turned"].made(ins)
                if not first:
                    rw_var()
                for h in range(2):
                    r = slice(64 * h, 64 * h + 64)
                    for g, (g0, n) in enumerate(GROUPS):
                        ins = nc.tensor.matmul(ps[0:n, h, g0:g0 + n], rar[r, 0, g0:g0 + n], rbk[r, 0, g0:g0 + n], start=True, stop=True)
                t["rw_plain"].made(ins)
            def pair(more):
                t["rw_state_put"].next(pe)
                for g, (g0, n) in enumerate(GROUPS):
                    if g == 1:
                        t["rw_tok"].next(pe, 3)
                        t["rw_bkx"].next(pe, 3)
                    for h in range(2):
                        r = slice(64 * h, 64 * h + 64)
                        for j in range(2):
                            out = ps[0:n, 2 + 2 * g + h, 256 * j:256 * j + 256].rearrange("p (a t) -> p a t", a=2)[:, :, 0:n]
                            ins = nc.tensor.matmul(out, rbk[r, j, g0:g0 + n], rar[r, :, g0:g0 + n], start=True, stop=True)
                    t["rw_scores"].made(ins)
                t["rw_scored"].next(pe)
                if more:
                    rw_block(0)
                t["rw_scored"].next(pe, 2)
                t["rw_q"].next(pe)

                def square(level, g, n, both):
                    for h in range(2):
                        if level == 0:
                            plain, turned = rpw[0:n, 0, g, h, 0, 0:n], rsc[0:n, g, h, 0, 0:n]
                        else:
                            plain, turned = (rpw[0:n, level % 2, g, h, x, 0:n] for x in range(2))
                        ins = nc.tensor.matmul(ps[0:n, 2 + g, 256 * h:256 * h + n], turned, plain, start=True, stop=True)
                        if both:
                            ins = nc.tensor.matmul(ps[0:n, 2 + g, 256 * h + 128:256 * h + 128 + n], plain, turned, start=True, stop=True)
                    t["rw_squared"].made(ins)

                for g, (g0, n) in enumerate(GROUPS):
                    square(0, g, n, True)
                if more:
                    rw_block(1)
                for level in range(1, 5):
                    t["rw_power"].next(pe, 3)
                    if level > 1:
                        t["rw_grown"].next(pe, 3)
                    for g, (g0, n) in enumerate(GROUPS):
                        for h in range(2):
                            ins = nc.tensor.matmul(ps[0:n, 5 + g, P * h:P * h + n], rpw[0:n, level % 2, g, h, 0, 0:n],
                                                   rq[0:n, (level - 1) % 2, g, h, 0:n], start=True, stop=True)
                        t["rw_grow"].made(ins)
                        if level < 4:
                            square(level, g, n, level < 3)
                    if more and level == 1:
                        t["rw_evac"].next(pe)
                        rw_block(2)
                if more:
                    t["rw_evac"].next(pe, 2)
                for g, (g0, n) in enumerate(GROUPS):
                    for h in range(2):
                        ins = nc.tensor.matmul(ps[0:n, 0, (2 * g + h) * 64:(2 * g + h + 1) * 64], rsc[0:n, g, h, 1, 0:n],
                                               rvt[0:n, g, 64 * h:64 * h + 64], start=True, stop=True)
                t["rw_akv"].made(ins)
                t["rw_x"].next(pe)
                t["rw_grown"].next(pe, 3)
                for g, (g0, n) in enumerate(GROUPS):
                    for h in range(2):
                        b, c0 = ((1, 0), (1, 256), (0, 0))[g]
                        ins = nc.tensor.matmul(ps[0:n, b, c0 + P * h:c0 + P * h + P], rq[0:n, 0, g, h, 0:n],
                                               rax[0:n, g, h, :, :], start=True, stop=True)
                t["rw_gh"].made(ins)
                if more:
                    rw_keys()
                t["rw_ghs"].next(pe)
                t["rw_bonus"].made(nc.tensor.matmul(ps[:, 1, 0:T], K("heads"), rbonus[:, :], start=True, stop=True))
                for g, (g0, n) in enumerate(GROUPS):
                    nch = n // C
                    for h in range(2):
                        r = slice(64 * h, 64 * h + 64)
                        nc.tensor.matmul(ps[r, 2 + g, 0:64 * nch], rgh[0:n, g, h, 0:64], rbx[0:n, g, 0:nch, r], start=True, stop=True)
                        for c in range(nch):
                            out = ps[r, 2 + g, 256 + 64 * c:320 + 64 * c]
                            nc.tensor.matmul(out, rbx[0:n, g, c, r], rgh[0:n, g, h, 64:128], start=True, stop=False)
                            ins = nc.tensor.matmul(out, rkx[0:n, g, c, r], rvt[0:n, g, r], start=False, stop=True)
                    t["rw_mn"].made(ins)
                for g, (g0, n) in enumerate(GROUPS):
                    for h in range(2):
                        r = slice(64 * h, 64 * h + 64)
                        ins = nc.tensor.matmul(ps[r, 5, g0:g0 + n], rgh[0:n, g, h, 0:64], rsc[0:n, g, h, 0, 128:128 + n], start=True, stop=True)
                t["rw_z"].made(ins)
                for g, (g0, n) in enumerate(GROUPS):
                    for h in range(2):
                        r = slice(64 * h, 64 * h + 64)
                        nc.tensor.matmul(ps[r, 6, g0:g0 + n], rgh[0:n, g, h, 64:128], rsc[0:n, g, h, 0, 128:128 + n], start=True, stop=False, skip_group_check=True)
                        ins = nc.tensor.matmul(ps[r, 6, g0:g0 + n], rvt[0:n, g, r], rsc[0:n, g, h, 1, 128:128 + n], start=False, stop=True, skip_group_check=True)
                t["rw_yi"].made(ins)
                t["rw_mns"].next(pe, 3)
                for c in (8, 1, 2, 3, 4, 5, 6, 7):
                    if c != 8:
                        t["rw_state"].next(pe, 2 if c == 2 else 1)
                    t["rw_step"].made(nc.tensor.matmul(ps[:, 2 if c == 8 else 0, 0:P], rmt[:, c, :], rst[:, c if c < 8 else 9, :], start=True, stop=True))
                t["rw_state"].next(pe)
                t["rw_zs"].next(pe)
                for c in range(NCH):
                    ins = nc.tensor.matmul(ps[:, 4, c * C:(c + 1) * C], rst[:, c if c < 8 else 9, :], rz[:, c * C:(c + 1) * C], start=True, stop=True)
                t["rw_ys"].made(ins)
                for s2, slot in enumerate((8, 10)):
                    ins = nc.tensor.transpose(ps[:, 2 + s2, 0:P], rst[:, slot, :], K("ident"))
                t["rw_final"].made(ins)
                t["rw_y"].next(pe)
                t["rw_mean"].made(nc.tensor.matmul(ps[:, 4, 0:T], K("heads"), rt[:, 0, :], start=True, stop=True))
                if more:
                    rw_front(False)
                else:
                    rw_var()
                t["rw_root"].next(pe)

            rw_block(0)
            rw_block(1)
            t["rw_evac"].next(pe)
            rw_block(2)
            t["rw_evac"].next(pe, 2)
            rw_keys()
            rw_front(True)
            with pe.Fori(0, 3) as i:
                enter(i, RW_PER, 3)
                pair(True)
            leave(3, RW_PER)
            pair(False)
            t["shifts_turned"].made(nc.tensor.transpose(ps[0:28, 0, 0:P], shiftb[:, :, :].rearrange("p s j -> p (s j)"), K("ident")))
            t["mixed"].next(pe)
            for j in range(4):
                s = take()
                for c in range(2):
                    b = 2 * j + c
                    if b >= 4:
                        pe.wait_ge(sem["abo_added"], b - 3)
                    ins = gemm(ps[:, 1 + b % 4, 0:T], s, 128 * c, 256, yT)
                    t["unit_used" if c else "first_block"].made(ins)

            pe.wait_ge(sem["abo_added"], 8)
            norm()

            def ffn_up(first, fresh=False):
                for b in range(4):
                    if not first:
                        t["ffn_silu" if b < 2 else "ffn_made"].next(pe)
                    if b % 2 == 0:
                        s = take()
                    t["unit_used" if b % 2 else "first_block"].made(gemm(ps[:, b, 0:T], s, 128 * (b % 2), 256, hT, fresh=fresh and b == 0))

            ffn_up(True, True)
            ffn_up(False)
            with pe.Fori(0, 3) as i:
                enter(i, FFN_PER, 6)
                for q in range(3):
                    ffn_up(False)
            leave(3, FFN_PER)

            def ffn_down(k, half, first, last):
                s = take()
                w = ring[:, s, 0:1024].rearrange("p (k n) -> p k n", k=2)
                for x in range(2):
                    for n in range(4):
                        ins = nc.tensor.matmul(ps[:, 4 - 4 * half + n, 0:T], w[:, x, n * P:(n + 1) * P], gT[:, k + x, :],
                                               start=first and x == 0, stop=last and x == 1)
                t["unit_used"].made(ins)
                return ins

            t["ffn_made"].next(pe, 2)
            for half in range(2):
                ffn_down(0, half, True, False)
                with pe.Fori(0, 3) as i:
                    enter(i, DOWN_PER, 3)
                    for q in range(3):
                        ffn_down(i * 6 + (2 + 2 * q), half, False, False)
                leave(3, DOWN_PER)
                ffn_down(20, half, False, True)
            pe.wait_ge(sem["ffn_added"], 8)
            norm()

            def ret_mean():
                t["ret_osb"].next(pe)
                for j in range(4):
                    ins = nc.tensor.matmul(ps[:, 7, 0:T], K("ones"), ro[:, j, :], start=j == 0, stop=j == 3)
                t["ret_mean"].made(ins)

            def ret_var():
                t["ret_osq"].next(pe)
                for j in range(4):
                    ins = nc.tensor.matmul(ps[:, 6, 0:T], K("ones"), rosq[:, j, :], start=j == 0, stop=j == 3)
                t["ret_var"].made(ins)

            def head(first):
                for b in range(12):
                    if b >= 2:
                        t["ret_evac"].wait(pe, b - 1)
                    if b % 2 == 0:
                        s = take()
                    t["unit_used" if b % 2 else "first_block"].made(gemm(ps[:, b % 2, 0:T], s, 128 * (b % 2), 256, hT, fresh=first and b == 0))
                    if b == 1 and not first:
                        ret_mean()
                    if b == 3 and not first:
                        ret_var()
                    if b == 8:
                        t["ret_evac"].wait(pe, 8)
                        if not first:
                            t["ret_root"].next(pe)
                        for g, (g0, n) in enumerate(GROUPS):
                            for j in range(4):
                                ins = nc.tensor.transpose(ps[0:n, 4 + g, j * P:(j + 1) * P], rvf[:, j, g0:g0 + n], K("ident"))
                        t["ret_vturned"].made(ins)
                        t["ret_rotated"].next(pe)
                        for g, (g0, n) in enumerate(GROUPS):
                            for j in range(2):
                                ins = nc.tensor.transpose(ps[0:n, 2 + g // 2, (2 * (g % 2) + j) * P:(2 * (g % 2) + j + 1) * P], rrot[:, 2 + j, g0:g0 + n], K("ident"))
                        t["ret_kturned"].made(ins)
                    if b == 9:
                        for out, ks, qs in ((ps[:, 7, 0:256], slice(0, 128), slice(0, 256)), (ps[:, 7, 256:384], slice(128, 256), slice(128, 256)),
                                            (ps[0:TS, 7, 384:416], slice(TP, T), slice(TP, T))):
                            for j in range(2):
                                ins = nc.tensor.matmul(out, rrot[:, 2 + j, ks], rrot[:, j, qs], start=j == 0, stop=j == 1)
                        t["ret_scores"].made(ins)
                t["ret_vtok"].next(pe)
                t["ret_ktok"].next(pe)
                for x in range(2):
                    c = slice(x * P, (x + 1) * P)
                    nc.tensor.matmul(ps[:, 2 + x, :], rK[:, 0, c], rV[:, 0, :], start=True, stop=False)
                    nc.tensor.matmul(ps[:, 2 + x, :], rK[:, 1, c], rV[:, 1, :], start=False, stop=True)
                t["ret_evac"].next(pe, 12)
                for x in range(2):
                    ins = nc.tensor.matmul(ps[:, x, :], rK[0:TS, 2, x * P:(x + 1) * P], rV[0:TS, 2, :], start=True, stop=True)
                t["ret_states"].made(ins)
                t["ret_att"].next(pe)
                t["ret_state_in"].next(pe, 16)
                for j in range(4):
                    c = slice(j * P, (j + 1) * P)
                    nc.tensor.matmul(ps[:, 4 + j, 0:256], rV[:, 0, c], ratt[:, 0:256], start=True, stop=False, skip_group_check=True)
                    nc.tensor.matmul(ps[:, 4 + j, 128:256], rV[:, 1, c], ratt[:, 256:384], start=False, stop=True, skip_group_check=True)
                    nc.tensor.matmul(ps[:, 4 + j, 256:T], rV[0:TS, 2, c], ratt[0:TS, 384:416], start=True, stop=False, skip_group_check=True)
                    for x in range(2):
                        ins = nc.tensor.matmul(ps[:, 4 + j, 256:T], rS0[:, x, c], rqs[:, x, :], start=False, stop=x == 1, skip_group_check=True)
                t["ret_o"].made(ins)
                t["ret_stated_p"].next(pe)
                t["ret_stated_s"].next(pe)

            head(True)
            with pe.Fori(0, 3) as i:
                enter(i, RET_PER, 6)
                head(False)
            leave(3, RET_PER)
            for half in range(2):
                for kh in range(2):
                    for j in (2 * half, 2 * half + 1):
                        s = take()
                        for c in range(2):
                            b = 2 * j + c
                            if b >= 4 and kh == 0:
                                pe.wait_ge(sem["reto_added"], b - 3)
                            ins = gemm(ps[:, b % 4, 0:T], s, 128 * c, 256, yR[:, KD * kh:KD * kh + KD, :], start=kh == 0, stop=kh == 1)
                            t["unit_used" if c else "first_block"].made(ins)
                        if j == 0 and kh == 0:
                            ret_mean()
                        if j == 1 and kh == 0:
                            ret_var()
                            t["ret_done"].wait(pe, 1)
            pe.wait_ge(sem["reto_added"], 8)
            norm()
            for g, (g0, n) in enumerate(GROUPS):
                for k in range(KD):
                    if g == 0:
                        t["normed"].next(pe)
                    ins = nc.tensor.matmul(ps[0:n, 0, 8 * g:8 * g + 8], hT[:, k, g0:g0 + n], w_router[:, k, :], start=k == 0, stop=k == KD - 1)
                if g == 0:
                    t["slot_free"].made(ins, RINGX)
            t["logits"].made(ins)
            for g, (g0, n) in enumerate(GROUPS):
                for k in range(KD):
                    ins = nc.tensor.transpose(ps[0:n, 1 + 2 * g + k // 4, (k % 4) * P:(k % 4 + 1) * P], hT[:, k, g0:g0 + n], K("ident"))
            t["frames_turned"].made(ins)
            t["picked"].next(pe)
            for g, (g0, n) in enumerate(GROUPS):
                for g2 in range(g):
                    nc.tensor.matmul(ps[0:n, 7, 8 * g:8 * g + 8], K("ones", 0, n), pick[:, g2, 0:NEXP], start=g2 == 0, stop=False)
                nc.tensor.matmul(ps[0:n, 7, 8 * g:8 * g + 8], K("before", 0, n)[0:n], pick[0:n, g, 0:NEXP], start=g == 0, stop=True)
            for g, (g0, n) in enumerate(GROUPS):
                ins = nc.tensor.matmul(ps[:, 7, 32:40], K("ones")[0:n], pick[0:n, g, 0:NEXP], start=g == 0, stop=g == 2)
            t["placed"].made(ins)
            pe.wait_ge(sem["rounds_known"], 1)
            pe.wait_ge(sem["frames_tok"], 1)
            def gather():
                for k in range(KD):
                    for g, (g0, n) in enumerate(GROUPS):
                        ins = nc.tensor.matmul(ps[:, 4 + k // 4, (k % 4) * CAP:(k % 4 + 1) * CAP], htok[0:n, g, k * P:(k + 1) * P], take_f[0:n, g, :], start=g == 0, stop=g == 2)
                t["x_taken"].made(ins)

            def scatter(k):
                if k >= 2:
                    t["x_added"].next(pe)
                t["x_out"].made(nc.tensor.matmul(ps[:, 4 + k % 2, 0:T], yx[:, k * P:(k + 1) * P], giveT[:, :], start=True, stop=True))

            t["x_give"].next(pe)
            gather()
            n_rounds = count_rounds(pe)
            with pe.Fori(0, n_rounds) as r:
                with pe.Fori(0, NEXP) as e:
                    turn = r * NEXP + e
                    enter(turn, X_PER, 33)

                    def x_take(k):
                        pe.wait_ge(x_arrived[k % RINGX], turn * 48 + 16 * (k // RINGX + 1))
                        return k % RINGX

                    t["x_h"].next(pe)
                    for j in range(KF // 2):
                        for x in range(2):
                            s = x_take(2 * j + x)
                            w = xring[:, s, :].rearrange("p (k n) -> p k n", k=KD)
                            if x == 0 and j >= 2:
                                t["x_read"].next(pe)
                            for c in range(2):
                                for k in range(KD):
                                    ins = nc.tensor.matmul(ps[:, 2 * (j % 2) + x, c * CAP:(c + 1) * CAP], w[:, k, c * P:(c + 1) * P], hx[:, k, :], start=k == 0, stop=k == KD - 1)
                            t["slot_free"].made(ins)
                        if j == 1:
                            t["x_y"].next(pe)
                        if 1 <= j <= 4:
                            scatter(2 * j - 2)
                            scatter(2 * j - 1)
                    t["x_added"].next(pe, 2)
                    t["x_read"].next(pe)
                    t["x_give"].next(pe)
                    for g, (g0, n) in enumerate(GROUPS):
                        ins = nc.tensor.transpose(ps[0:CAP, 2, g0:g0 + n], give_f[0:n, g, :], K("ident", 0, n)[0:n])
                    gather()
                    for j in range(KF // 2):
                        s = x_take(22 + j)
                        w = xring[:, s, :].rearrange("p (k n) -> p k n", k=2)
                        if j == 0:
                            t["x_read"].next(pe)
                        for x in range(2):
                            for c in range(2):
                                ins = nc.tensor.matmul(ps[0:CAP, 6 + c, :], gx_[:, 2 * j + x, :], w[:, x, 512 * c:512 * c + 512], start=j == 0 and x == 0, stop=j == 10 and x == 1)
                        t["slot_free"].made(ins)
            for name in X_PER:
                t[name].k = 0
            enter(n_rounds * NEXP, X_PER, 33)
            t["x_h"].next(pe)
            t["x_y"].next(pe)
            for k in range(KD):
                scatter(k)
            t["x_added"].next(pe, 2)
            pe.wait_ge(sem["x_ready"], 4)
            norm()
            for g, (g0, n) in enumerate(GROUPS):
                for k in range(KD):
                    if g == 0:
                        t["normed"].next(pe)
                    ins = nc.tensor.transpose(ps[0:n, 1 + 2 * g + k // 4, (k % 4) * P:(k % 4 + 1) * P], hT[:, k, g0:g0 + n], K("ident"))
                t["y_turned"].made(ins)

        @block.scalar
        def _(act):
            t = {n: Tally(s, n) for n, s in sem.items()}
            A = nc.scalar.activation

            def enter(i, per):
                for n, p in per.items():
                    t[n].enter(i, p)

            def leave(n, per):
                for name in per:
                    t[name].leave(n)

            def norm(r):
                t["x_ready"].next(act)
                for k in (0, 4):
                    t["squares"].made(A(yT[:, k:k + 4, :], xT[:, k:k + 4, :], ACT.Square))
                t["square_sums"].next(act)
                t["roots"].made(A(rstd[:, 0, :], ps[:, 7, 0:T], ACT.Sqrt, bias=eps(EPS), scale=1.0 / D))

            for n, (name, _w) in enumerate(ROWS):
                at, w = VEC[name]
                src = a[name]
                while len(src.shape) > 2:
                    src = src[0]
                if len(src.shape) == 2:
                    src = src.rearrange("a n -> (a n)") if src.shape[0] > 1 and name != "rwkv_r_k" else (src.rearrange("a n -> (a n)"))
                act.dma_start(rows[at % P:at % P + w, at // P, :], src.rearrange("(j p) -> j p", p=P)).then_inc(sem["in_rows"], 16)
            act.dma_start(const[:, 256:], a["const"][:, 256:]).then_inc(sem["in_const"], 16)
            act.dma_start(w_ga[:, :, :], W_IN[:, :, GA:GA + 16]).then_inc(sem["in_lora"], 16)
            act.dma_start(w_gate[:, :], a["gla_w_gate2"][0]).then_inc(sem["in_lora"], 16)
            act.dma_start(w_wa[0:64, :], a["rwkv_w2"][0]).then_inc(sem["in_lora"], 16)
            act.dma_start(w_wa[64:128, :], a["rwkv_a2"][0]).then_inc(sem["in_lora"], 16)
            act.dma_start(w_g[:, :], a["rwkv_g2"][0]).then_inc(sem["in_lora"], 16)
            act.dma_start(w_router[:, :, :], a["moe_router"][0].rearrange("(k p) e -> p k e", p=P)).then_inc(sem["in_lora"], 16)
            act.dma_start(gla_in[:, :, :], a["state_gla"][0, 0].rearrange("(q h) k v -> (h k) q v", q=2)).then_inc(sem["in_lora"], 16)
            act.dma_start(rw_in[:, :, :], a["state_rwkv"][0, 0].rearrange("(q h) v k -> (h v) q k", q=4)).then_inc(sem["in_lora"], 16)

            act.wait_ge(sem["eps_set"], 1)
            for k in range(KD):
                t["x_turned"].next(act)
                ins = A(xT[:, k, :], ps[:, 2 + k % 4, 0:T], ACT.Copy)
                t["x_copied"].made(ins)
            act.wait_ge(sem["x_copied"], KD)
            for k in (0, 4):
                t["squares"].made(A(yT[:, k:k + 4, :], xT[:, k:k + 4, :], ACT.Square))
            t["square_sums"].next(act)
            t["roots"].made(A(rstd[:, 0, :], ps[:, 7, 0:T], ACT.Sqrt, bias=eps(EPS), scale=1.0 / D))

            t["first_block"].next(act)
            t["unit_used"].next(act)
            A(lora[:, 0:2, :], ps[:, 0:2, 0:T], ACT.Copy)
            t["lora_raw"].made(A(lora[:, 2:4, 1:T], ps[:, 0:2, 0:T - 1], ACT.Copy))
            t["ga_block"].next(act)
            t["gate_in"].made(A(gaT[:, :], ps[0:16, 2, 0:T], ACT.Copy))
            t["lora_shifted"].next(act)
            A(lora[0:64, 4, :], lora[0:64, 4, :], ACT.Tanh)
            t["lora_in"].made(A(lora[:, 5, :], lora[:, 5, :], ACT.Sigmoid))
            for j in range(4):
                t["lora_mixed"].next(act)
                b = 3 * (j % 2)
                if j == 1:
                    act.wait_ge(sem["gate_out"], 1)
                A(lw[:, j, :], ps[:, b, 0:T], ACT.Sigmoid, bias=V("rwkv_w0", j))
                A(av[:, j, :], ps[:, b + 1, 0:T], ACT.Sigmoid, bias=V("rwkv_a0", j))
                t["lora_out"].made(A(gv[:, j, :], ps[:, b + 2, 0:T], ACT.Copy))
            t["gate_out"].next(act)
            t["act_chain"].link(act, A(gz[:, 1], gz[:, 0], ACT.Abs))
            t["act_chain"].link(act, A(gz[:, 1], gz[:, 1], ACT.Exp, scale=-1.0))
            t["gate_log"].made(A(gz[:, 1], gz[:, 1], ACT.Ln, bias=one()))
            t["gate_sums"].next(act)
            A(gexp[:, 0], gz[:, 1], ACT.Exp)
            A(gexp[:, 1], gz[:, 1], ACT.Exp, scale=-1.0)
            A(gexp[:, 2], gz[:, 0], ACT.Exp)
            A(gexp[:, 3], gz[:, 2], ACT.Exp)
            t["gate_exps"].made(A(gend[:, :, :], gz[:, 0].rearrange("p q (c t) -> p q c t", t=C)[:, :, :, C - 1], ACT.Exp))
            t["decay_sums"].next(act)
            A(rexp[:, 0], lw[:, :, :], ACT.Exp)
            A(rexp[:, 2], lw[:, :, :], ACT.Exp, scale=-1.0)
            t["decay_exps"].made(A(rexp[:, 1], rexp[:, 1], ACT.Exp))

            with act.Fori(0, 2) as i:
                enter(i, GLA_PER)
                for b in range(6):
                    t["unit_used"].next(act)
                    if b == 0 or b == 2 or b == 4:
                        pass
                    ins = A(gx[:, b, :], ps[:, b % 2, 0:T], ACT.Copy, scale=0.125 if b == 0 else 1.0)
                    t["gla_evac"].made(ins)
                t["gla_evac"].wait(act)
                t["gla_og"].made(A(go[:, 2:4, :], gx[:, 4:6, :], ACT.Sigmoid))
                for g, (g0, n) in enumerate(GROUPS):
                    t["gla_turned"].next(act)
                    t["gla_kx"].next(act)
                    t["gla_vt"].made(A(gvt[0:n, g, :, :], ps[0:n, 4 + g, P:3 * P].rearrange("p (h v) -> p h v", h=2), ACT.Copy))
                t["gla_o"].next(act)
                A(go[:, 0, :], ps[:, 6, 0:T], ACT.Square)
                t["gla_osq"].made(A(go[:, 1, :], ps[:, 2, 0:T], ACT.Square))
                t["gla_osum"].next(act)
                t["gla_root"].made(A(go[:, 0:2, :], ps[:, 3:5, 0:T], ACT.Sqrt, bias=eps(EPS), scale=1.0 / P))
                t["gla_read"].next(act)
            leave(2, GLA_PER)

            def rw_block(b):
                t["unit_used"].next(act)
                A(rx[:, b, :], ps[:, b % 2, 0:T], ACT.Copy)
                t["rw_evac"].made(A(rp[:, b, 1:T], ps[:, b % 2, 0:T - 1], ACT.Copy))

            def rw_root():
                t["rw_ksum"].next(act)
                t["rw_kroot"].made(A(rt[:, 2, :], ps[:, 7, 0:T], ACT.Sqrt))

            def rw_norm_root():
                t["rw_var"].next(act)
                t["rw_root"].made(A(rt[:, 2, :], ps[:, 4, 0:T], ACT.Sqrt, bias=eps(64e-5), scale=1.0 / 64))

            def rw_front(first):
                t["rw_state_turned"].next(act)
                t["rw_state_put"].made(A(rst[:, 9, :], ps[:, 3, 0:P], ACT.Copy))
                if not first:
                    rw_norm_root()
                for g, (g0, n) in enumerate(GROUPS):
                    t["rw_turned"].next(act)
                    t["rw_bkx"].next(act)
                    A(rax[0:n, g, :, 0, :], ps[0:n, 5 + g, 0:P].rearrange("p (h k) -> p h k", h=2), ACT.Copy)
                    t["rw_tok"].made(A(rvt[0:n, g, :], ps[0:n, 5 + g, 3 * P:4 * P], ACT.Copy))

            def pair(p, more):
                if more:
                    rw_block(0)
                for level in range(1, 5):
                    for g, (g0, n) in enumerate(GROUPS):
                        t["rw_squared"].next(act)
                        src = ps[0:n, 2 + g, :].rearrange("p (h a t) -> p h a t", h=2, a=2)
                        x = 2 if level < 4 else 1
                        for h in range(2):
                            ins = A(rpw[0:n, level % 2, g, h, 0:x, 0:n], src[:, h, 0:x, 0:n], ACT.Copy)
                        t["rw_power"].made(ins)
                    if more and level < 3:
                        rw_block(level)
                t["rw_akv"].next(act)
                A(rax[:, 0:2, :, 1, :], ps[:, 0, 0:256].rearrange("p (g h v) -> p g h v", g=2, h=2), ACT.Copy)
                t["rw_x"].made(A(rax[0:TS, 2, :, 1, :], ps[0:TS, 0, 256:384].rearrange("p (h v) -> p h v", h=2), ACT.Copy))
                t["rw_gh"].next(act)
                A(rgh[:, 0:2, :, :], ps[:, 1, :].rearrange("p (g h v) -> p g h v", g=2, h=2), ACT.Copy)
                t["rw_ghs"].made(A(rgh[0:TS, 2, :, :], ps[0:TS, 0, 0:256].rearrange("p (h v) -> p h v", h=2), ACT.Copy))
                if more:
                    rw_root()
                t["rw_yi"].next(act)
                t["rw_yis"].made(A(ryi[:, :], ps[:, 6, 0:T], ACT.Copy))
                t["rw_final"].next(act)
                A(rw_out[0:64, p, :, :], ps[0:64, 2:4, 0:64], ACT.Copy)
                t["rw_out"].made(A(rw_out[64:128, p, :, :], ps[64:128, 2:4, 64:P], ACT.Copy))
                t["rw_centred"].next(act)
                t["rw_ysq"].made(A(rt[:, 1, :], rt[:, 0, :], ACT.Square))
                if more:
                    rw_front(False)
                else:
                    rw_norm_root()

            for b in range(3):
                rw_block(b)
            rw_root()
            rw_front(True)
            with act.Fori(0, 3) as i:
                enter(i, RW_PER)
                pair(i, True)
            leave(3, RW_PER)
            pair(3, False)
            t["shifts_turned"].next(act)
            t["shifts_out"].made(A(shifto[:, :], ps[0:28, 0, 0:P], ACT.Copy))

            act.wait_ge(sem["abo_added"], 8)
            norm(1)
            t["first_block"].k += 4
            t["unit_used"].k += 4

            def ffn_up(first):
                for b in range(2):
                    t["unit_used" if b else "first_block"].next(act)
                    if not first:
                        t["ffn_made"].next(act)
                    t["ffn_silu"].made(A(fsil[:, b, :], ps[:, b, 0:T], ACT.Silu))
                t["unit_used"].k += 1
                t["first_block"].k += 1

            ffn_up(True)
            ffn_up(False)
            with act.Fori(0, 3) as i:
                enter(i, FFN_PER)
                for q in range(3):
                    ffn_up(False)
            leave(3, FFN_PER)
            act.wait_ge(sem["ffn_added"], 8)
            norm(2)
            t["unit_used"].k += 22

            def ret_squares():
                t["ret_centred"].next(act)
                t["ret_osq"].made(A(rosq[:, :, :], ro[:, :, :], ACT.Square))

            def ret_root():
                t["ret_var"].next(act)
                t["ret_root"].made(A(rstd[:, 0, :], ps[:, 6, 0:T], ACT.Sqrt, bias=eps(1e-5), scale=1.0 / 512))

            def head(first):
                for b in range(12):
                    if b == 8 and not first:
                        t["ret_done"].next(act)
                    t["unit_used" if b % 2 else "first_block"].next(act)
                    dst = (rqk, rvf, rgf)[b // 4][:, b % 4, :]
                    t["ret_evac"].made(A(dst, ps[:, b % 2, 0:T], ACT.Silu if b >= 8 else ACT.Copy))
                    if b == 1 and not first:
                        ret_squares()
                    if b == 3 and not first:
                        ret_root()
                    if b == 8:
                        t["ret_vturned"].next(act)
                        A(rV[:, 0:2, :], ps[:, 4:6, :], ACT.Copy)
                        t["ret_vtok"].made(A(rV[0:TS, 2, :], ps[0:TS, 6, :], ACT.Copy))
                t["ret_states"].next(act)
                t["ret_buffer"].next(act)
                t["ret_stated_p"].made(A(rS[:, 0, :, :], ps[:, 2:4, :], ACT.Copy))
                t["ret_o"].next(act)
                t["ret_osb"].made(A(ro[:, :, :], ps[:, 4:8, 0:T], ACT.Copy))

            head(True)
            with act.Fori(0, 3) as i:
                enter(i, RET_PER)
                head(False)
            leave(3, RET_PER)
            ret_squares()
            ret_root()
            act.wait_ge(sem["reto_added"], 8)
            norm(3)
            act.wait_ge(sem["ret_stored"], 32 * 4)
            t["logits_centred"].next(act)
            for g, (g0, n) in enumerate(GROUPS):
                ins = A(prob[0:n, g, :], prob[0:n, g, :], ACT.Exp)
            t["logits_exp"].made(ins)
            t["frames_turned"].next(act)
            for g, (g0, n) in enumerate(GROUPS):
                ins = A(htok[0:n, g, :], ps[0:n, 1 + 2 * g:3 + 2 * g, :].rearrange("p a n -> p (a n)"), ACT.Copy)
            t["frames_tok"].made(ins)
            act.wait_ge(sem["rounds_known"], 1)
            t["slot_free"].k = RINGX
            def keep_frames():
                for x in range(2):
                    ins = A(hx[:, 4 * x:4 * x + 4, :], ps[:, 4 + x, 0:4 * CAP].rearrange("p (k n) -> p k n", k=4), ACT.Copy)
                t["x_h"].made(ins)

            t["x_taken"].next(act)
            keep_frames()
            with act.Fori(0, count_rounds(act)) as r:
                with act.Fori(0, NEXP) as e:
                    enter(r * NEXP + e, X_PER)
                    for j in range(KF // 2):
                        t["slot_free"].next(act)
                        if j >= 2:
                            t["x_read"].next(act)
                        t["x_silu"].made(A(xsil[:, j % 2, :], ps[:, 2 * (j % 2), 0:2 * CAP], ACT.Silu))
                        t["slot_free"].k += 1
                    t["x_read"].k += 2
                    t["x_taken"].next(act)
                    A(giveT[:, :], ps[0:CAP, 2, 0:T], ACT.Copy)
                    keep_frames()
                    t["slot_free"].next(act, 11)
                    A(yx[:, 0:512], ps[0:CAP, 6, :], ACT.Copy)
                    t["x_y"].made(A(yx[:, 512:D], ps[0:CAP, 7, :], ACT.Copy))
            norm(4)
            for g, (g0, n) in enumerate(GROUPS):
                t["y_turned"].next(act)
                ins = A(ytok[0:n, g, :], ps[0:n, 1 + 2 * g:3 + 2 * g, :].rearrange("p a n -> p (a n)"), ACT.Copy)
                t["y_copied"].made(ins)
                act.wait_ge(sem["y_copied"], g + 1)
                act.dma_start(o[0][0, g0:g0 + n, :] if g < 2 else o[1][0], ytok[0:n, g, :]).then_inc(sem["y_stored"], 16)
            act.wait_ge(sem["y_stored"], 16 * 3)

        @block.vector
        def _(dve):
            t = {n: Tally(s, n) for n, s in sem.items()}
            v = nc.vector

            def enter(i, per):
                for n, p in per.items():
                    t[n].enter(i, p)

            def leave(n, per):
                for name in per:
                    t[name].leave(n)

            def link(ins):
                t["dve_chain"].link(dve, ins)

            def tt(out, x, y, op=ALU.mult):
                return v.tensor_tensor(out, x, y, op)

            def stt(out, x, s, y, op0, op1):
                return v.scalar_tensor_tensor(out=out, in0=x, scalar=s, in1=y, op0=op0, op1=op1)

            def norm(r):
                t["roots"].next(dve)
                link(v.reciprocal(rstd[:, 1, :], rstd[:, 0, :]))
                w = norm_columns(r)
                for k in range(KD):
                    t["normed"].made(stt(hT[:, k, :], xT[:, k, :], w[:, k:k + 1], rstd[:, 1, :], ALU.mult, ALU.mult))

            v.memset(epsb[:, 0:1], EPS)
            v.memset(epsb[:, 1:2], 64e-5)
            v.memset(epsb[:, 2:3], 1.0)
            t["eps_set"].made(v.memset(epsb[:, 3:4], 1e-5))
            v.memset(gst[:, 0, :], 0.0)
            link(v.memset(lora[:, 2:4, 0:1], 0.0))
            t["vec_turned"].next(dve)
            v.tensor_copy(vec[:, 0:99], ps[:, 0, 0:99])
            link(v.tensor_copy(vec[:, P:P + 32], ps[:, 1, 0:32]))
            v.tensor_scalar(omka[:, :], V("rwkv_k_a", 0, 4), -1.0, 1.0, ALU.mult, ALU.add)
            norm(0)

            t["lora_raw"].next(dve)
            for j in range(2):
                v.tensor_copy(lora[:, 2 + j, TP:TP + 1], V("state_shift", 12 + j))
            for s2, col in enumerate((TP - 1, T - 1)):
                ins = v.tensor_copy(shiftb[:, s2, 12:14], lora[:, 0:2, col])
            link(ins)
            link(tt(lora[:, 2:4, :], lora[:, 2:4, :], lora[:, 0:2, :], ALU.subtract))
            for j in range(2):
                ins = stt(lora[:, 4 + j, :], lora[:, 2 + j, :], V("rwkv_mu", 12 + j), lora[:, j, :], ALU.mult, ALU.add)
            t["lora_shifted"].made(ins)
            dve.wait_ge(sem["in_const"], 16)
            t["gate_blocks"].next(dve)
            for j in range(2):
                ins = v.tensor_scalar(gz[:, 0, j, :], ps[:, 3 + j, 0:T], V("gla_b_gate", j), None, ALU.add)
            t["gate_out"].made(ins)
            t["gate_out"].wait(dve)
            link(v.tensor_scalar(gz[:, 2], gz[:, 0], 0.0, None, ALU.min))
            t["gate_log"].next(dve)
            link(tt(gz[:, 2], gz[:, 2], gz[:, 1], ALU.subtract))
            link(v.tensor_scalar(gz[:, 2], gz[:, 2], 1.0 / 16, None, ALU.mult))
            for j in range(2):
                ins = v.tensor_tensor_scan(gz[:, 0, j, :], K("scan"), gz[:, 2, j, :], 0.0, ALU.mult, ALU.add)
            link(ins)
            for j in range(2):
                b = chunks(gz[:, 0, j, :])
                last = b[:, :, C - 1:C].to_broadcast([P, NCH, C])
                stt(chunks(gz[:, 1, j, :]), last, -0.5, b, ALU.mult, ALU.add)
                ins = tt(chunks(gz[:, 2, j, :]), last, b, ALU.subtract)
            t["gate_sums"].made(ins)
            t["lora_out"].next(dve, 4)
            link(v.tensor_scalar(rexp[:, 0], lw[:, :, :], -float(np.exp(-0.5)), None, ALU.mult))
            for j in range(4):
                ins = v.tensor_tensor_scan(lw[:, j, :], K("scan"), rexp[:, 0, j, :], 0.0, ALU.mult, ALU.add)
            link(ins)
            link(tt(rexp[:, 1], lw[:, :, :], rexp[:, 0], ALU.subtract))
            t["decay_sums"].made(v.memset(epsb[:, 4:5], 0.0))

            t["gate_exps"].next(dve)
            dve.wait_ge(sem["in_lora"], 16 * SMALL_LOADS)
            with dve.Fori(0, 2) as i:
                enter(i, GLA_PER)
                t["gla_evac"].k += 1
                t["gla_evac"].next(dve)
                tt(gf[:, 0, :], gx[:, 0, :], gexp[:, 0, i, :])
                tt(gf[:, 1, :], gx[:, 1, :], gexp[:, 1, i, :])
                tt(gf[:, 2, :], gx[:, 0, :], gexp[:, 2, i, :])
                t["gla_feats"].made(tt(gf[:, 3, :], gx[:, 1, :], gexp[:, 3, i, :]))
                v.tensor_copy(gst[:, 9, :], gla_in[:, i, :])
                t["gla_scores"].next(dve)
                tt(gatt[:, :, 0:256], ps[:, 2:4, 0:256], K("incl_t").unsqueeze(1).to_broadcast([P, 2, 256]))
                t["gla_masked"].made(tt(gatt[0:TS, :, 256:T], ps[0:TS, 2:4, 256:T], K("incl_t", 0, TS)[0:TS].unsqueeze(1).to_broadcast([TS, 2, TS])))
                for g, (g0, n) in enumerate(GROUPS):
                    t["gla_turned"].next(dve)
                    nch = n // C
                    t["gla_kx"].made(tt(gkx[0:n, g, 0:nch, :], ps[0:n, 4 + g, 0:P].unsqueeze(1).to_broadcast([n, nch, P]),
                                        K("chunk", 0, nch)[0:n].unsqueeze(2).to_broadcast([n, nch, P])))
                for g, b in ((0, 7), (1, 4), (2, 5)):
                    t["gla_updates"].next(dve)
                    for c in range(GROUPS[g][1] // C):
                        cc = 4 * g + c
                        src, dst = (cc, cc + 1) if cc < 8 else (9, 10)
                        link(stt(gst[:, dst, :], gst[:, src, :], gend[:, i, cc:cc + 1], ps[:, b, c * P:(c + 1) * P], ALU.mult, ALU.add))
                v.tensor_copy(gla_out[:, i, 0, :], gst[:, 8, :])
                t["gla_states"].made(v.tensor_copy(gla_out[:, i, 1, :], gst[:, 10, :]))
                t["gla_evac"].next(dve, 4)
                t["gla_og"].next(dve)
                link(tt(go[:, 2:4, :], go[:, 2:4, :], gx[:, 4:6, :]))
                t["gla_root"].next(dve)
                link(v.reciprocal(gf[:, 0:2, :], go[:, 0:2, :]))
                for h, b in ((0, 6), (1, 2)):
                    ins = stt(gf[:, 2 + h, :], ps[:, b, 0:T], V("gla_norm"), gf[:, h, :], ALU.mult, ALU.mult)
                link(ins)
                t["gla_read"].made(tt(yT[:, bass.ds(i * 2, 2), :], gf[:, 2:4, :], go[:, 2:4, :]))
            leave(2, GLA_PER)

            t["decay_exps"].next(dve)
            v.memset(rst[:, 0, :], 0.0)
            v.memset(rsi[:, :], 0.0)
            v.memset(rmt[:, :, :], 0.0)
            link(v.memset(rnw[:, :, :], 0.0))
            def pro_shift(p):
                t["rw_evac"].next(dve, 3)
                v.memset(rp[:, :, 0:1], 0.0)
                for b in range(3):
                    v.tensor_copy(rp[:, b, TP:TP + 1], vec[:, bass.ds(p + (VEC["state_shift"][0] + 4 * b), 1)])
                    v.tensor_copy(shiftb[:, 0, bass.ds(p + 4 * b, 1)], rx[:, b, TP - 1:TP])
                    ins = v.tensor_copy(shiftb[:, 1, bass.ds(p + 4 * b, 1)], rx[:, b, T - 1:T])
                link(ins)
                link(tt(rp[:, :, :], rp[:, :, :], rx[:, :, :], ALU.subtract))

            def pro_mix(p):
                for b in range(3):
                    ins = stt(rsh[:, b, :], rp[:, b, :], vec[:, bass.ds(p + (VEC["rwkv_mu"][0] + 4 * b), 1)], rx[:, b, :], ALU.mult, ALU.add)
                link(ins)
                link(v.tensor_scalar(rt[:, 0, :], rsh[:, 1, :], vec[:, bass.ds(p + VEC["rwkv_k_k"][0], 1)], None, ALU.mult))
                t["rw_ksq"].made(tt(rt[:, 1, :], rt[:, 0, :], rt[:, 0, :]))

            def pro_key(p):
                link(v.tensor_scalar(rt[:, 4, :], av[:, p, :], vec[:, bass.ds(p + VEC["rwkv_k_a"][0], 1)], omka[:, bass.ds(p, 1)], ALU.mult, ALU.add))
                link(tt(rkn[:, :], rt[:, 4, :], rsh[:, 1, :]))
                tt(rar[:, 1, :], rsh[:, 0, :], rexp[:, 0, p, :])
                tt(rbk[:, 1, :], rkn[:, :], rexp[:, 2, p, :])

            def pro_inverse():
                t["rw_kroot"].next(dve)
                link(v.tensor_scalar(rt[:, 2, :], rt[:, 2, :], 1e-12, None, ALU.max))
                link(v.reciprocal(rt[:, 3, :], rt[:, 2, :]))

            def pro_kk(p):
                link(tt(rt[:, 1, :], rt[:, 0, :], rt[:, 3, :]))
                stt(rar[:, 0, :], rt[:, 1, :], -1.0, rexp[:, 1, p, :], ALU.mult, ALU.mult)
                link(tt(rt[:, 2, :], rt[:, 1, :], av[:, p, :]))
                t["rw_feats"].made(tt(rbk[:, 0, :], rt[:, 2, :], rexp[:, 2, p, :]))

            def rw_front(p):
                v.tensor_copy(rsi[0:64, 0:64], rw_in[0:64, p, :])
                t["rw_state_in"].made(v.tensor_copy(rsi[64:128, 64:128], rw_in[64:128, p, :]))
                for g, (g0, n) in enumerate(GROUPS):
                    nch = n // C
                    t["rw_turned"].next(dve)
                    for j, dst in enumerate((rbx, rkx)):
                        ins = tt(dst[0:n, g, 0:nch, :], ps[0:n, 5 + g, (1 + j) * P:(2 + j) * P].unsqueeze(1).to_broadcast([n, nch, P]),
                                 K("chunk", 0, nch)[0:n].unsqueeze(2).to_broadcast([n, nch, P]))
                    t["rw_bkx"].made(ins)
                t["rw_plain"].next(dve)
                for h in range(2):
                    for g, (g0, n) in enumerate(GROUPS):
                        tt(rpw[0:n, 0, g, h, 0, 0:n], ps[0:n, h, g0:g0 + n], K("strict", 0, n)[0:n])

            def pair(p, more):
                for g, (g0, n) in enumerate(GROUPS):
                    t["rw_scores"].next(dve)
                    mask = K("strict_incl_t")[0:n].rearrange("p (a t) -> p a t", a=2)[:, :, 0:n]
                    for h in range(2):
                        src = ps[0:n, 2 + 2 * g + h, :].rearrange("p (b a t) -> p b a t", b=2, a=2)[:, :, :, 0:n]
                        dst = rsc[0:n, g, h, :, :].rearrange("p b (a t) -> p b a t", a=2)[:, :, :, 0:n]
                        for b in range(2):
                            ins = tt(dst[:, b], src[:, b], mask)
                    t["rw_scored"].made(ins)
                t["rw_scored"].wait(dve)
                for g, (g0, n) in enumerate(GROUPS):
                    ins = tt(rq[0:n, 0, g, :, 0:n], rsc[0:n, g, :, 0, 0:n], K("ident", 0, n)[0:n].unsqueeze(1).to_broadcast([n, 2, n]), ALU.add)
                t["rw_q"].made(ins)
                stt(rbonus[:, :], rsh[:, 0, :], vec[:, bass.ds(p + VEC["rwkv_r_k"][0], 1)], rkn[:, :], ALU.mult, ALU.mult)
                v.tensor_copy(rkeep[:, 0, :], rsh[:, 2, :])
                link(v.tensor_copy(rkeep[:, 1, :], rar[:, 1, :]))
                t["rw_q"].wait(dve)
                for level in range(1, 5):
                    for g, (g0, n) in enumerate(GROUPS):
                        t["rw_grow"].next(dve)
                        src = ps[0:n, 5 + g, 0:256].rearrange("p (h t) -> p h t", h=2)[:, :, 0:n]
                        t["rw_grown"].made(tt(rq[0:n, level % 2, g, :, 0:n], src, rq[0:n, (level - 1) % 2, g, :, 0:n], ALU.add))
                    t["rw_grown"].wait(dve)
                    if more and level == 2:
                        pro_shift(p + 1)
                    if more and level == 3:
                        pro_mix(p + 1)
                    if more and level == 4:
                        pro_key(p + 1)
                for g, (g0, n) in enumerate(GROUPS):
                    nch, c0 = n // C, g0 // C
                    t["rw_mn"].next(dve)
                    m = ps[:, 2 + g, :].rearrange("p (x c v) -> p x c v", x=2, c=4)
                    for h in range(2):
                        r = slice(64 * h, 64 * h + 64)
                        tt(rmt[r, c0:c0 + nch, r], m[r, 0, 0:nch, :], K("ident64")[r].unsqueeze(1).to_broadcast([64, nch, 64]), ALU.add)
                        wl = rexp[r, 0, p, :].rearrange("p (c t) -> p c t", t=C)[:, c0:c0 + nch, C - 1:C].to_broadcast([64, nch, 64])
                        ins = tt(rnw[r, c0:c0 + nch, r], m[r, 1, 0:nch, :], wl)
                    t["rw_mns"].made(ins)
                t["rw_mns"].wait(dve)
                t["rw_state"].made(v.tensor_copy(rst[:, 1, :], rnw[:, 0, :]))
                for c in (8, 1, 2, 3, 4, 5, 6, 7):
                    t["rw_step"].next(dve)
                    t["rw_state"].made(stt(rst[:, c + 1 if c < 8 else 10, :], ps[:, 2 if c == 8 else 0, 0:P],
                                           rexp[:, 0, p, c * C + C - 1:c * C + C], rnw[:, c, :], ALU.mult, ALU.add))
                    if c == 5:
                        t["rw_bonus"].next(dve)
                        link(tt(rt[:, 4, :], ps[:, 1, 0:T], rkeep[:, 0, :]))
                    if more and c == 1:
                        pro_inverse()
                    if more and c == 3:
                        pro_kk(p + 1)
                t["rw_z"].next(dve)
                t["rw_zs"].made(tt(rz[:, :], ps[:, 5, 0:T], rkeep[:, 1, :], ALU.add))
                t["rw_ys"].next(dve)
                t["rw_yis"].next(dve)
                t["rw_y"].made(tt(rt[:, 0, :], ps[:, 4, 0:T], ryi[:, :], ALU.add))
                t["rw_mean"].next(dve)
                t["rw_centred"].made(stt(rt[:, 0, :], ps[:, 4, 0:T], -1.0 / 64, rt[:, 0, :], ALU.mult, ALU.add))
                if more:
                    rw_front(p + 1)
                t["rw_root"].next(dve)
                t["rw_centred"].wait(dve)
                link(v.reciprocal(rt[:, 3, :], rt[:, 2, :]))
                link(tt(rt[:, 0, :], rt[:, 0, :], rt[:, 3, :]))
                link(v.tensor_scalar(rt[:, 0, :], rt[:, 0, :], vec[:, bass.ds(p + VEC["rwkv_gn_g"][0], 1)],
                                     vec[:, bass.ds(p + VEC["rwkv_gn_b"][0], 1)], ALU.mult, ALU.add))
                link(tt(rt[:, 0, :], rt[:, 0, :], rt[:, 4, :], ALU.add))
                link(tt(yT[:, bass.ds(p + 4, 1), :], rt[:, 0:1, :], gv[:, bass.ds(p, 1), :]))

            pro_shift(0)
            pro_mix(0)
            pro_key(0)
            pro_inverse()
            pro_kk(0)
            rw_front(0)
            with dve.Fori(0, 3) as i:
                enter(i, RW_PER)
                pair(i, True)
            leave(3, RW_PER)
            pair(3, False)
            t["mixed"].made(v.memset(epsb[:, 4:5], 0.0))
            for b in range(8):
                t["unit_used" if b % 2 else "first_block"].k += 1
                dve.wait_ge(sem["first_block"], 2 + b // 2)
                if b % 2:
                    dve.wait_ge(sem["unit_used"], 1 + 12 + 12 + b // 2 + 1)
                ins = tt(xT[:, b, :], ps[:, 1 + b % 4, 0:T], xT[:, b, :], ALU.add)
                t["abo_added"].made(ins)
            t["x_ready"].made(v.memset(epsb[:, 4:5], 0.0))
            norm(1)
            t["first_block"].k = 1 + 4
            t["unit_used"].k, t["unit_used"].base = 29, 0

            def ffn_up(pair):
                t["first_block"].k += 1
                t["unit_used"].k += 1
                for b in range(2):
                    t["ffn_silu"].next(dve)
                    t["unit_used" if b else "first_block"].next(dve)
                    t["ffn_made"].made(tt(gT[:, bass.ds(pair * 2 + b, 1), :], fsil[:, b:b + 1, :], ps[:, 2 + b:3 + b, 0:T]))

            ffn_up(0)
            ffn_up(1)
            with dve.Fori(0, 3) as i:
                enter(i, FFN_PER)
                for q in range(3):
                    ffn_up(i * 3 + (2 + q))
            leave(3, FFN_PER)
            for half in range(2):
                t["unit_used"].next(dve, 11)
                for n in range(4):
                    t["ffn_added"].made(tt(xT[:, 4 * half + n, :], ps[:, 4 - 4 * half + n, 0:T], xT[:, 4 * half + n, :], ALU.add))
            t["x_ready"].made(v.memset(epsb[:, 4:5], 0.0))
            norm(2)

            def ret_norm(h):
                t["ret_mean"].next(dve)
                t["ret_osb"].next(dve)
                t["ret_centred"].made(stt(ro[:, :, :], ps[:, 7, 0:T].unsqueeze(1).to_broadcast([P, 4, T]), -1.0 / 512, ro[:, :, :], ALU.mult, ALU.add))
                t["ret_root"].next(dve)
                link(v.reciprocal(rstd[:, 1, :], rstd[:, 0, :]))
                t["ret_centred"].wait(dve)
                link(tt(ro[:, :, :], ro[:, :, :], rstd[:, 1, :].unsqueeze(1).to_broadcast([P, 4, T])))
                for j in range(4):
                    ins = v.tensor_scalar(ro[:, j, :], ro[:, j, :], vec[:, bass.ds(h(4, VEC["ret_gn_g"][0] + j), 1)],
                                          vec[:, bass.ds(h(4, VEC["ret_gn_b"][0] + j), 1)], ALU.mult, ALU.add)
                link(ins)
                t["ret_done"].made(tt(yR[:, bass.ds(h(4, 0), 4), :], ro[:, :, :], rgf[:, :, :]))

            def head(h, last):
                if last is not None:
                    ret_norm(last)
                t["ret_evac"].next(dve, 4)
                cs, sn = (K(x).unsqueeze(1).to_broadcast([P, 2, T]) for x in ("cos", "sin"))
                qk = rqk[:, :, :].rearrange("p (a b) t -> p a b t", a=2)
                rot = rrot[:, :, :].rearrange("p (a b) t -> p a b t", a=2)
                tmp = rrt[:, :, :].rearrange("p (a b) t -> p a b t", a=2)
                tt(rot[:, :, 0], qk[:, :, 0], cs)
                tt(rot[:, :, 1], qk[:, :, 1], cs)
                tt(tmp[:, :, 0], qk[:, :, 1], sn)
                link(tt(tmp[:, :, 1], qk[:, :, 0], sn))
                tt(rot[:, :, 0], rot[:, :, 0], tmp[:, :, 0], ALU.subtract)
                link(tt(rot[:, :, 1], rot[:, :, 1], tmp[:, :, 1], ALU.add))
                c0 = const_layout()[0]["ret_q"][0]
                dec = const[:, bass.ds(h(32, c0), 32)].unsqueeze(1).to_broadcast([P, 2, TS])
                t["ret_rotated"].made(tt(rqs[:, :, :], rrot[:, 0:2, TP:T], dec))
                t["ret_kturned"].next(dve)
                c0 = const_layout()[0]["ret_k"][0]
                for g, (g0, n) in enumerate(GROUPS):
                    ins = v.tensor_scalar(rK[0:n, g, :], ps[0:n, 2 + g // 2, 256 * (g % 2):256 * (g % 2) + 256],
                                          const[0:n, bass.ds(h(1, c0 + 4 * g), 1)], None, ALU.mult)
                t["ret_ktok"].made(ins)
                t["ret_scores"].next(dve)
                c0 = const_layout()[0]["ret_mask"][0]
                m = [const[:, bass.ds(h(256, c0), n)] for n in (256, 128)]
                tt(ratt[:, 0:256], ps[:, 7, 0:256], m[0])
                tt(ratt[:, 256:384], ps[:, 7, 256:384], m[1])
                t["ret_att"].made(tt(ratt[0:TS, 384:416], ps[0:TS, 7, 384:416], const[0:TS, bass.ds(h(256, c0), TS)]))
                t["ret_evac"].next(dve, 8)
                t["ret_states"].next(dve)
                t["ret_state_in"].next(dve, 16)
                t["ret_buffer"].next(dve)
                c0 = const_layout()[0]["ret_q"][0]
                t["ret_stated_s"].made(stt(rS[:, 1, :, :], rS0[:, :, :], const[:, bass.ds(h(32, c0 + 31), 1)], ps[:, 0:2, :], ALU.mult, ALU.add))

            head(lambda w, c: c, None)
            t["unit_used"].k += 6
            with dve.Fori(0, 3) as i:
                enter(i, RET_PER)
                head(lambda w, c: i * w + (w + c), lambda w, c: i * w + c)
            leave(3, RET_PER)
            ret_norm(lambda w, c: 3 * w + c)
            for half in range(2):
                t["unit_used"].next(dve, 2)
                for b in range(4 * half, 4 * half + 4):
                    if b % 2 == 0:
                        t["unit_used"].next(dve, 1)
                    t["reto_added"].made(tt(xT[:, b, :], ps[:, b % 4, 0:T], xT[:, b, :], ALU.add))
            t["x_ready"].made(v.memset(epsb[:, 4:5], 0.0))
            dve.wait_ge(sem["ret_stored"], 32 * 4)
            norm(3)
            t["logits"].next(dve)
            for g, (g0, n) in enumerate(GROUPS):
                ins = v.tensor_reduce(small[0:n, g:g + 1], ps[0:n, 0, 8 * g:8 * g + 8], AX_X, ALU.max)
            link(ins)
            for g, (g0, n) in enumerate(GROUPS):
                ins = v.tensor_scalar(prob[0:n, g, :], ps[0:n, 0, 8 * g:8 * g + 8], small[0:n, g:g + 1], None, ALU.subtract)
            t["logits_centred"].made(ins)
            t["logits_exp"].next(dve)
            for g, (g0, n) in enumerate(GROUPS):
                ins = v.tensor_reduce(small[0:n, 3 + g:4 + g], prob[0:n, g, :], AX_X, ALU.add)
            link(ins)
            for g, (g0, n) in enumerate(GROUPS):
                ins = v.reciprocal(small[0:n, 6 + g:7 + g], small[0:n, 3 + g:4 + g])
            link(ins)
            for g, (g0, n) in enumerate(GROUPS):
                ins = v.tensor_scalar(prob[0:n, g, :], prob[0:n, g, :], small[0:n, 6 + g:7 + g], None, ALU.mult)
            link(ins)
            for g, (g0, n) in enumerate(GROUPS):
                ins = v.max(top[0:n, g, :], prob[0:n, g, :])
            link(ins)
            for g, (g0, n) in enumerate(GROUPS):
                ins = v.max_index(topi[0:n, g, :], top[0:n, g, :], prob[0:n, g, :])
            link(ins)
            for g, (g0, n) in enumerate(GROUPS):
                ins = v.tensor_copy(topf[0:n, g, 0:2], topi[0:n, g, 0:2])
            link(ins)
            for g, (g0, n) in enumerate(GROUPS):
                v.tensor_scalar(pick[0:n, g, 0:NEXP], K("cols", 0, 8)[0:n], topf[0:n, g, 0:1], None, ALU.is_equal)
                ins = v.tensor_scalar(gate[0:n, g, :], K("cols", 0, 8)[0:n], topf[0:n, g, 1:2], None, ALU.is_equal)
            link(ins)
            for g, (g0, n) in enumerate(GROUPS):
                ins = tt(pick[0:n, g, 0:NEXP], pick[0:n, g, 0:NEXP], gate[0:n, g, :], ALU.add)
                tt(small[0:n, 9 + g:10 + g], top[0:n, g, 0:1], top[0:n, g, 1:2], ALU.add)
            t["picked"].made(v.memset(epsb[:, 4:5], 0.0))
            t["picked"].wait(dve)
            for g, (g0, n) in enumerate(GROUPS):
                ins = v.reciprocal(small[0:n, 12 + g:13 + g], small[0:n, 9 + g:10 + g])
            link(ins)
            for g, (g0, n) in enumerate(GROUPS):
                ins = stt(gate[0:n, g, :], prob[0:n, g, :], small[0:n, 12 + g:13 + g], pick[0:n, g, 0:NEXP], ALU.mult, ALU.mult)
            link(ins)
            t["placed"].next(dve)
            for g, (g0, n) in enumerate(GROUPS):
                v.tensor_copy(place[0:n, g, 0:NEXP], ps[0:n, 7, 8 * g:8 * g + 8])
                v.tensor_scalar(place[0:n, g, NEXP:NEXP + 1], ps[0:n, 7, 8 * g:8 * g + 1], float(CAP), None, ALU.subtract)
                v.tensor_copy(pick[0:n, g, NEXP:NEXP + 1], pick[0:n, g, 0:1])
            link(v.tensor_reduce(small[:, 0:1], ps[:, 7, 32:40], AX_X, ALU.max))
            link(v.tensor_scalar(small[:, 1:2], small[:, 0:1], float(CAP), 1.0, ALU.is_gt, ALU.add))
            link(stt(small[:, 2:3], small[:, 0:1], 2.0 * CAP, small[:, 1:2], ALU.is_gt, ALU.add))
            t["rounds_known"].made(v.tensor_copy(rounds[0:1, 0:1], small[0:1, 2:3]))
            t["rounds_known"].wait(dve)
            t["slot_free"].k = RINGX
            def take(e):
                for g, (g0, n) in enumerate(GROUPS):
                    ins = v.tensor_scalar(take_f[0:n, g, :], K("cols", 0, CAP)[0:n], place[0:n, g, bass.ds(e, 1)], pick[0:n, g, bass.ds(e, 1)], ALU.is_equal, ALU.mult)
                return ins

            def add(k):
                t["x_out"].next(dve)
                t["x_added"].made(tt(xT[:, k, :], ps[:, 4 + k % 2, 0:T], xT[:, k, :], ALU.add))

            t["x_give"].made(take(0))
            t["x_taken"].k += 1
            v.memset(yx[:, :], 0.0)
            t["x_y"].made(v.memset(giveT[:, :], 0.0))
            n_rounds = count_rounds(dve)
            with dve.Fori(0, n_rounds) as r:
                with dve.Fori(0, NEXP) as e:
                    enter(r * NEXP + e, X_PER)
                    t["x_taken"].wait(dve)
                    for g, (g0, n) in enumerate(GROUPS):
                        v.tensor_scalar(give_f[0:n, g, :], K("cols", 0, CAP)[0:n], place[0:n, g, bass.ds(e, 1)], gate[0:n, g, bass.ds(e, 1)], ALU.is_equal, ALU.mult)
                    t["x_give"].made(take(e + 1))
                    for j in range(KF // 2):
                        t["x_silu"].next(dve)
                        t["slot_free"].next(dve, 2)
                        t["x_read"].made(tt(gx_[:, 2 * j:2 * j + 2, :], xsil[:, j % 2, :].rearrange("p (c n) -> p c n", c=2),
                                            ps[:, 2 * (j % 2) + 1, 0:2 * CAP].rearrange("p (c n) -> p c n", c=2)))
                        if 1 <= j <= 4:
                            add(2 * j - 2)
                            add(2 * j - 1)
                    t["slot_free"].k += 11
                for g, (g0, n) in enumerate(GROUPS):
                    ins = v.tensor_scalar(place[0:n, g, :], place[0:n, g, :], float(CAP), None, ALU.subtract)
                ins.then_inc(sem["places_moved"], 1)
                dve.wait_ge(sem["places_moved"], r + 1)
            for name in X_PER:
                t[name].k = 0
            enter(n_rounds * NEXP, X_PER)
            for k in range(KD):
                add(k)
            t["x_ready"].made(v.memset(epsb[:, 4:5], 0.0))
            norm(4)

        @block.gpsimd
        def _(pool):
            pool.wait_ge(sem["gla_read"], 2)
            pool.wait_ge(sem["gla_states"], 2)
            pool.wait_ge(sem["rw_out"], 4)
            pool.wait_ge(sem["shifts_out"], 1)
            for s2, (og, orw, osh) in enumerate(((o[2], o[3], o[4]), (o[6], o[7], o[8]))):
                pool.dma_start(og[0, 0].rearrange("(q h) k v -> (h k) q v", q=2), gla_out[:, :, s2, :]).then_inc(sem["stored"], 16)
                pool.dma_start(orw[0, 0].rearrange("(q h) v k -> (h v) q k", q=4), rw_out[:, :, s2, :]).then_inc(sem["stored"], 16)
                pool.dma_start(osh[0, 0].rearrange("a (j p) -> (a j) p", p=P), shifto[14 * s2:14 * s2 + 14, :]).then_inc(sem["stored"], 16)
            pool.wait_ge(sem["normed"], 3 * KD)
            pool.dma_start(rS0[:, :, :], a["state_ret"][0, 0, 0].rearrange("(x k) v -> k x v", x=2)).then_inc(sem["ret_state_in"], 16)
            pool.sem_inc(sem["ret_buffer"], 1)

            def store(i):
                for s2, dst in enumerate((o[5], o[9])):
                    pool.dma_start(dst[0, 0, bass.ds(i, 1)][0].rearrange("(x k) v -> k x v", x=2), rS[:, s2, :, :]).then_inc(sem["ret_stored"], 16)

            with pool.Fori(0, 3) as i:
                pool.wait_ge(sem["ret_stated_p"], i + 1)
                pool.wait_ge(sem["ret_stated_s"], i + 1)
                store(i)
                pool.wait_ge(sem["ret_o"], i + 1)
                pool.dma_start(rS0[:, :, :], a["state_ret"][0, 0, bass.ds(i + 1, 1)][0].rearrange("(x k) v -> k x v", x=2)).then_inc(sem["ret_state_in"], 16)
                pool.wait_ge(sem["ret_stored"], i * 32 + 32)
                pool.sem_inc(sem["ret_buffer"], 1)
            pool.wait_ge(sem["ret_stated_p"], 4)
            pool.wait_ge(sem["ret_stated_s"], 4)
            store(3)
            pool.wait_ge(sem["stored"], 16 * 6)
            pool.wait_ge(sem["ret_stored"], 32 * 4)


_OUTS = [(1, TP, D), (1, TS, D), (1, 1, 4, 64, 128), (1, 1, 8, 64, 64), (1, 1, 1, 1792), (1, 1, 4, 256, 512),
         (1, 1, 4, 64, 128), (1, 1, 8, 64, 64), (1, 1, 1, 1792), (1, 1, 4, 256, 512)]


def kernel(**inputs):
    import concourse.bacc as bacc
    from concourse.bass_utils import run_bass_kernel_spmd

    nc = bacc.Bacc("TRN2", target_bir_lowering=False, num_devices=1)
    arrays, args = {}, {}
    for name, value in inputs.items():
        arr = np.ascontiguousarray(value)
        arrays[f"in_{name}"] = arr
        args[name] = nc.dram_tensor(f"in_{name}", arr.shape, F32, kind="ExternalInput").ap()
    arrays["in_const"] = const_array()
    args["const"] = nc.dram_tensor("in_const", arrays["in_const"].shape, F32, kind="ExternalInput").ap()
    outs = [nc.dram_tensor(f"out_{i}", shape, F32, kind="ExternalOutput").ap() for i, shape in enumerate(_OUTS)]
    program(nc, args, outs)
    r = run_bass_kernel_spmd(nc, [arrays], core_ids=[0])
    return tuple(r.results[0][f"out_{i}"] for i in range(len(_OUTS)))
```
